# Optimizing a Trainium2 kernel written in Bass

```python
import math
import jax, jax.numpy as jnp
from jax import lax
import numpy as np

D_MODEL = 2048
BATCH = 1
SEQ = 256
DEPTH = 1

N_MIXERS = 2
N_A = (DEPTH + N_MIXERS - 1) // N_MIXERS
N_B = DEPTH // N_MIXERS
HEAD_DIM = 64
N_MAPS = D_MODEL // HEAD_DIM
DA_HEADS = N_MAPS // 2
DA_VDIM = 2 * HEAD_DIM
SW_Q_HEADS = N_MAPS
SW_KV_HEADS = 4
SW_WINDOW = 128
BLOCK = 128
NUM_BUCKETS = 32
MAX_DISTANCE = 128
D_FF = 5632
CONV_WIDTH = 3
EPS = 1e-6

kernel_name = "hybrid_diffattn_swa_sink_convffn"

def rms_norm(x, g):
    xf = x.astype(jnp.float32)
    y = xf * lax.rsqrt(jnp.mean(xf * xf, axis=-1, keepdims=True) + EPS)
    return (y * g.astype(jnp.float32)).astype(x.dtype)

def t5_bucket(dist):
    max_exact = NUM_BUCKETS // 2
    d = jnp.maximum(dist, 0)
    df = jnp.maximum(d, 1).astype(jnp.float32)
    large = max_exact + (jnp.log(df / max_exact) / math.log(MAX_DISTANCE / max_exact)
                         * (NUM_BUCKETS - max_exact)).astype(jnp.int32)
    large = jnp.minimum(large, NUM_BUCKETS - 1)
    return jnp.where(d < max_exact, d, large)

def diff_attention(h, w_qkv, w_o, q_gain, k_gain, lq1, lk1, lq2, lk2, sub_gain, rel_table, layer_idx):
    B, S, _ = h.shape
    qkv = h @ w_qkv
    q, k, v = jnp.split(qkv, [DA_HEADS * 2 * HEAD_DIM, 2 * DA_HEADS * 2 * HEAD_DIM], axis=-1)
    q = rms_norm(q.reshape(B, S, DA_HEADS, 2, HEAD_DIM), q_gain) * (HEAD_DIM ** -0.5)
    k = rms_norm(k.reshape(B, S, DA_HEADS, 2, HEAD_DIM), k_gain)
    v = v.reshape(B, S, DA_HEADS, DA_VDIM)
    lam_init = 0.8 - 0.6 * math.exp(-0.3 * layer_idx)
    f32 = jnp.float32
    lam = (jnp.exp(jnp.sum(lq1.astype(f32) * lk1.astype(f32)))
           - jnp.exp(jnp.sum(lq2.astype(f32) * lk2.astype(f32))) + lam_init)
    nb = S // BLOCK
    qb = q.reshape(B, nb, BLOCK, DA_HEADS, 2, HEAD_DIM).transpose(1, 0, 2, 3, 4, 5)
    key_pos = jnp.arange(S)

    def one_block(args):
        qblk, bi = args
        q_pos = bi * BLOCK + jnp.arange(BLOCK)
        dist = q_pos[:, None] - key_pos[None, :]
        bias = rel_table[t5_bucket(dist)].astype(f32)
        bias = bias.reshape(BLOCK, S, DA_HEADS, 2).transpose(2, 3, 0, 1)
        s = jnp.einsum('bqhmd,bkhmd->bhmqk', qblk, k).astype(f32) + bias
        s = jnp.where(dist >= 0, s, -jnp.inf)
        p = jax.nn.softmax(s, axis=-1)
        a = p[:, :, 0] - lam * p[:, :, 1]
        return jnp.einsum('bhqk,bkhe->bqhe', a.astype(v.dtype), v)

    o = lax.map(one_block, (qb, jnp.arange(nb)))
    o = o.transpose(1, 0, 2, 3, 4).reshape(B, S, DA_HEADS, DA_VDIM)
    o = rms_norm(o, sub_gain) * (1.0 - lam_init)
    return o.reshape(B, S, DA_HEADS * DA_VDIM) @ w_o

def swa_attention(h, w_qkv, w_o, q_gain, k_gain, sinks, rel_table):
    B, S, _ = h.shape
    G = SW_Q_HEADS // SW_KV_HEADS
    f32 = jnp.float32
    qkv = h @ w_qkv
    q, k, v = jnp.split(qkv, [SW_Q_HEADS * HEAD_DIM, (SW_Q_HEADS + SW_KV_HEADS) * HEAD_DIM], axis=-1)
    q = rms_norm(q.reshape(B, S, SW_KV_HEADS, G, HEAD_DIM), q_gain) * (HEAD_DIM ** -0.5)
    k = rms_norm(k.reshape(B, S, SW_KV_HEADS, HEAD_DIM), k_gain)
    v = v.reshape(B, S, SW_KV_HEADS, HEAD_DIM)
    nb = S // BLOCK
    qb = q.reshape(B, nb, BLOCK, SW_KV_HEADS, G, HEAD_DIM)

    def band(t):
        tp = jnp.pad(t, ((0, 0), (BLOCK, 0), (0, 0), (0, 0))).reshape(B, nb + 1, BLOCK, SW_KV_HEADS, HEAD_DIM)
        return jnp.concatenate([tp[:, :-1], tp[:, 1:]], axis=2)

    kb, vb = band(k), band(v)
    q_loc = jnp.arange(BLOCK) + BLOCK
    k_loc = jnp.arange(2 * BLOCK)
    dist = q_loc[:, None] - k_loc[None, :]
    in_window = (dist >= 0) & (dist < SW_WINDOW)
    key_ok = (jnp.arange(nb)[:, None] * BLOCK - BLOCK + k_loc[None, :]) >= 0
    mask = in_window[None] & key_ok[:, None, :]
    bias = rel_table[t5_bucket(dist)].astype(f32)
    bias = bias.reshape(BLOCK, 2 * BLOCK, SW_KV_HEADS, G).transpose(2, 3, 0, 1)
    s = jnp.einsum('bnqhgd,bnkhd->bnhgqk', qb, kb).astype(f32) + bias
    s = jnp.where(mask[None, :, None, None], s, -jnp.inf)
    sink = sinks.astype(f32).reshape(SW_KV_HEADS, G)[None, None, :, :, None, None]
    m = jnp.maximum(jnp.max(s, axis=-1, keepdims=True), sink)
    e = jnp.exp(s - m)
    p = e / (jnp.sum(e, axis=-1, keepdims=True) + jnp.exp(sink - m))
    o = jnp.einsum('bnhgqk,bnkhd->bnqhgd', p.astype(v.dtype), vb)
    return o.reshape(B, S, SW_Q_HEADS * HEAD_DIM) @ w_o

def conv_ffn(h, w_in, conv_w, conv_b, w_out):
    u = h @ w_in
    u = lax.conv_general_dilated(u, conv_w[:, None, :], window_strides=(1,),
                                 padding=[(CONV_WIDTH - 1, 0)],
                                 dimension_numbers=('NWC', 'WIO', 'NWC'),
                                 feature_group_count=2 * D_FF) + conv_b
    gate, up = jnp.split(u, 2, axis=-1)
    return (jax.nn.silu(gate) * up) @ w_out

def setup_inputs(seed: int = 0) -> dict:
    key = jax.random.key(seed)
    ks = jax.random.split(key, 23)

    def nrm(k, shape, scale):
        return jax.random.normal(k, shape, jnp.float32) * scale

    da_w = 2 * DA_HEADS * 2 * HEAD_DIM + DA_HEADS * DA_VDIM
    sw_w = (SW_Q_HEADS + 2 * SW_KV_HEADS) * HEAD_DIM
    return {
        "x": nrm(ks[0], (BATCH, SEQ, D_MODEL), 1.0),
        "rel_table": nrm(ks[1], (NUM_BUCKETS, N_MAPS), 0.5),
        "attn_norm_g": 1.0 + nrm(ks[2], (DEPTH, D_MODEL), 0.02),
        "ffn_norm_g": 1.0 + nrm(ks[3], (DEPTH, D_MODEL), 0.02),
        "da_w_qkv": nrm(ks[4], (N_A, D_MODEL, da_w), D_MODEL ** -0.5),
        "da_w_o": nrm(ks[5], (N_A, DA_HEADS * DA_VDIM, D_MODEL), (DA_HEADS * DA_VDIM) ** -0.5),
        "da_q_gain": 1.0 + nrm(ks[6], (N_A, HEAD_DIM), 0.02),
        "da_k_gain": 1.0 + nrm(ks[7], (N_A, HEAD_DIM), 0.02),
        "da_lam_q1": nrm(ks[8], (N_A, HEAD_DIM), 0.1),
        "da_lam_k1": nrm(ks[9], (N_A, HEAD_DIM), 0.1),
        "da_lam_q2": nrm(ks[10], (N_A, HEAD_DIM), 0.1),
        "da_lam_k2": nrm(ks[11], (N_A, HEAD_DIM), 0.1),
        "da_sub_gain": 1.0 + nrm(ks[12], (N_A, DA_VDIM), 0.02),
        "sw_w_qkv": nrm(ks[13], (N_B, D_MODEL, sw_w), D_MODEL ** -0.5),
        "sw_w_o": nrm(ks[14], (N_B, SW_Q_HEADS * HEAD_DIM, D_MODEL), (SW_Q_HEADS * HEAD_DIM) ** -0.5),
        "sw_q_gain": 1.0 + nrm(ks[15], (N_B, HEAD_DIM), 0.02),
        "sw_k_gain": 1.0 + nrm(ks[16], (N_B, HEAD_DIM), 0.02),
        "sw_sinks": nrm(ks[17], (N_B, SW_Q_HEADS), 1.0),
        "ffn_w_in": nrm(ks[18], (DEPTH, D_MODEL, 2 * D_FF), D_MODEL ** -0.5),
        "ffn_conv_w": nrm(ks[19], (DEPTH, CONV_WIDTH, 2 * D_FF), CONV_WIDTH ** -0.5),
        "ffn_conv_b": nrm(ks[20], (DEPTH, 2 * D_FF), 0.02),
        "ffn_w_out": nrm(ks[21], (DEPTH, D_FF, D_MODEL), D_FF ** -0.5),
    }

def reference(x, rel_table, attn_norm_g, ffn_norm_g, da_w_qkv, da_w_o, da_q_gain, da_k_gain,
              da_lam_q1, da_lam_k1, da_lam_q2, da_lam_k2, da_sub_gain, sw_w_qkv, sw_w_o,
              sw_q_gain, sw_k_gain, sw_sinks, ffn_w_in, ffn_conv_w, ffn_conv_b, ffn_w_out):
    h = x
    for i in range(DEPTH):
        a = rms_norm(h, attn_norm_g[i])
        j = i // N_MIXERS
        if i % N_MIXERS == 0:
            h = h + diff_attention(a, da_w_qkv[j], da_w_o[j], da_q_gain[j], da_k_gain[j],
                                   da_lam_q1[j], da_lam_k1[j], da_lam_q2[j], da_lam_k2[j],
                                   da_sub_gain[j], rel_table, i)
        else:
            h = h + swa_attention(a, sw_w_qkv[j], sw_w_o[j], sw_q_gain[j], sw_k_gain[j],
                                  sw_sinks[j], rel_table)
        f = rms_norm(h, ffn_norm_g[i])
        h = h + conv_ffn(f, ffn_w_in[i], ffn_conv_w[i], ffn_conv_b[i], ffn_w_out[i])
    return h


_drawn_inputs = setup_inputs


def setup_inputs(seed=0):
    import zlib

    import numpy as np

    out = dict(_drawn_inputs(seed))
    spreads = {}
    factors = {'ffn_norm_g': 4.816,
     'da_q_gain': 3.904,
     'da_k_gain': 4.201,
     'da_lam_k1': 8.0,
     'da_lam_q2': 8.0,
     'da_sub_gain': 4.448,
     'ffn_conv_b': 4.697}
    for name, (base, spread) in spreads.items():
        noise = np.random.default_rng([zlib.crc32(name.encode()), seed]).standard_normal(out[name].shape)
        drawn = base * np.exp(spread * noise) if base else spread * noise
        out[name] = __import__('jax').numpy.asarray(drawn.astype(out[name].dtype))
    for name, factor in factors.items():
        out[name] = (out[name] * factor).astype(out[name].dtype)
    return out
```

```python
from contextlib import ExitStack

import concourse.bass as bass
from concourse import mybir

F32 = mybir.dt.float32
F32R = mybir.dt.float32r
ALU = mybir.AluOpType
ACT = mybir.ActivationFunctionType
AX_X = mybir.AxisListType.X

P = 128
HEAD_DIM = 64
EPS = 1e-6
MASKED = -1e30
LAM_INIT = 0.2
BANK = 512
RAW_SLOTS = 8
SPLIT_SLOTS = 4
SUB = 1024


def build_layer(nc, x, rel_table, bucket_onehot, attn_norm_g, ffn_norm_g, w_qkv, w_o, q_gain, k_gain,
                lam_q1, lam_k1, lam_q2, lam_k2, sub_gain, w_in, conv_w, conv_b, w_out, out):
    S, D = x.shape[1], x.shape[2]
    NB = S // P
    KC = D // P
    MAPS = D // HEAD_DIM
    HEADS = MAPS // 2
    VD = 2 * HEAD_DIM
    FF = w_out.shape[1]
    FC = FF // P
    BUCKETS = rel_table.shape[0]
    TAPS = conv_w.shape[1]
    assert (S, D, VD, TAPS) == (2 * P, 2048, P, 3)

    QKV_GROUPS = HEADS // 2
    QW = 2 * VD
    FFN_BLOCKS = 4
    FFN_GROUPS = FC // FFN_BLOCKS
    HALF = D // 2
    O_BASE = QKV_GROUPS * KC
    IN_BASE = O_BASE + 2 * HEADS
    OUT_BASE = IN_BASE + FFN_GROUPS * KC
    assert not (O_BASE % RAW_SLOTS or IN_BASE % RAW_SLOTS or OUT_BASE % RAW_SLOTS or KC % RAW_SLOTS)
    PIECES = KC // 4
    GROUP_RSTD = NB * 8
    TABLE_W = S + P
    BIAS_PARTS = 4

    with ExitStack() as ctx:
        def sb(name, shape, dt=F32):
            return ctx.enter_context(nc.sbuf_tensor(name, shape, dt))

        def sem(name):
            return ctx.enter_context(nc.semaphore(name))

        resid = sb("resid", [P, NB, D])
        act_hi = sb("act_hi", [P, KC, S], F32R)
        act_lo = sb("act_lo", [P, KC, S], F32R)
        weight_raw = sb("weight_raw", [P, RAW_SLOTS, SUB])
        weight_hi = sb("weight_hi", [P, SPLIT_SLOTS, SUB], F32R)
        weight_lo = sb("weight_lo", [P, SPLIT_SLOTS, SUB], F32R)
        chunk_hi = sb("chunk_hi", [P, SPLIT_SLOTS, S], F32R)
        chunk_lo = sb("chunk_lo", [P, SPLIT_SLOTS, S], F32R)
        shared = sb("shared", [P, FC * S + D])
        pos_bias = shared[:, 0:MAPS * S].rearrange("p (m k) -> p m k", k=S)
        attn_out = shared[:, MAPS * S:MAPS * S + HEADS * S].rearrange("p (h t) -> p h t", t=S)
        hidden = shared[:, 0:FC * S].rearrange("p (c t) -> p c t", t=S)
        scaled = shared[:, FC * S:FC * S + D]
        work = sb("work", [P, 5120])
        qk = work[:, 0:1024].rearrange("p (b c) -> p b c", b=NB)
        qk_sq = work[:, 1024:2048]
        scores1 = work[:, 1024:2048].rearrange("p (j m k) -> p j m k", j=2, m=2)
        v_sb = work[:, 2048:2560].rearrange("p (b c) -> p b c", b=NB)
        qT = work[:, 2560:3072].rearrange("p (j t) -> p j t", j=2)
        kT = work[:, 3072:3584].rearrange("p (j t) -> p j t", j=2)
        scores0 = work[:, 3584:4096].rearrange("p (j m k) -> p j m k", j=2, m=2)
        probsT = work[:, 4096:4864].rearrange("p (j c q) -> p j c q", j=2, c=3)
        o_junk = work[:, 4864:5120]
        gain_all = work[:, 2048:2048 + D]
        norm_junk = work[:, 4096:5120]
        conv_rows = work[0:2 * FC, 0:(TAPS + 1) * P].rearrange("c (t p) -> c t p", p=P)
        onehot_sb = work[0:BUCKETS, 512:512 + S]
        bias_rows = work[0:MAPS, 768:768 + TABLE_W]
        pre_gate = work[:, 0:FFN_BLOCKS * S].rearrange("p (i t) -> p i t", t=S)
        pre_up = work[:, FFN_BLOCKS * S:2 * FFN_BLOCKS * S].rearrange("p (i t) -> p i t", t=S)
        head_out = sb("head_out", [P, 2, NB, VD])
        ident = sb("ident", [P, P])
        table_sb = sb("table_sb", [BUCKETS, MAPS])
        conv_cols = sb("conv_cols", [P, TAPS + 1, 2 * FC])
        gains = sb("gains", [P, 5])
        lam_vecs = sb("lam_vecs", [P, 4, HEAD_DIM])
        lam_prod = sb("lam_prod", [P, 2, HEAD_DIM])
        lam_dot = sb("lam_dot", [P, 2])
        lam_exp = sb("lam_exp", [P, 2])
        lam_diff = sb("lam_diff", [P, 1])
        neg_lam = sb("neg_lam", [P, 1])
        norm_sq = sb("norm_sq", [P, NB, 4])
        norm_sum = sb("norm_sum", [P, NB])
        norm_ms = sb("norm_ms", [P, NB])
        norm_rstd = sb("norm_rstd", [P, NB])
        power = sb("power", [P, GROUP_RSTD])
        eps = sb("eps", [P, GROUP_RSTD])
        qk_ss = sb("qk_ss", [P, GROUP_RSTD])
        qk_ms = sb("qk_ms", [P, GROUP_RSTD])
        qk_rstd = sb("qk_rstd", [P, GROUP_RSTD])
        neg_max = sb("neg_max", [P, 2, 4])
        exp_sum = sb("exp_sum", [P, 2, 4])
        coef = sb("coef", [P, 2, 4])
        o_ss = sb("o_ss", [P, 2, NB])
        o_ms = sb("o_ms", [P, 2, NB])
        o_rstd = sb("o_rstd", [P, 2, NB])

        psum = ctx.enter_context(nc.psum_tensor("psum", [P, 8, BANK], F32))
        ps_qkT = psum[:, 4, :]
        ps_o = psum[:, 4, 0:S].rearrange("p (b e) -> p b e", b=NB)
        ps_s1 = psum[:, 5:7, 0:S]
        ps_s0 = psum[:, 5:7, S:S + P]
        ps_pT = psum[:, 7, 0:3 * P].rearrange("p (c q) -> p c q", c=3)
        ps_oT = psum[:, 7, 0:S]
        bias_scratch = nc.dram_tensor("bias_scratch", [MAPS, TABLE_W], F32, kind="Internal").ap()

        bias_copies = nc.dram_tensor("bias_copies", [P, MAPS, TABLE_W], F32, kind="Internal").ap()

        raw_landed = [sem(f"raw_landed{i}") for i in range(RAW_SLOTS)]
        hi_ready = sem("hi_ready")
        lo_ready = sem("lo_ready")
        weights_used = sem("weights_used")
        chunk_hi_ready = sem("chunk_hi_ready")
        chunk_lo_ready = sem("chunk_lo_ready")
        x_landed = [sem(f"x_landed{b}") for b in range(NB)]
        gain_landed = [sem("attn_gain_landed"), sem("ffn_gain_landed")]
        small_landed = sem("small_landed")
        conv_landed = sem("conv_landed")
        table_landed = sem("table_landed")
        ident_zero = sem("ident_zero")
        ident_ready = sem("ident_ready")
        power_ready = sem("power_ready")
        mask_ready = sem("mask_ready")
        table_summed = sem("table_summed")
        table_stored = sem("table_stored")
        bias_written = sem("bias_written")
        bias_copied = [sem(f"bias_copied{i}") for i in range(BIAS_PARTS)]
        bias_landed = sem("bias_landed")
        conv_turned = sem("conv_turned")
        conv_stored = sem("conv_stored")
        gains_step = sem("gains_step")
        lam_step = sem("lam_step")
        lam_exped = sem("lam_exped")
        norm_squared = sem("norm_squared")
        norm_summed = sem("norm_summed")
        norm_ms_ready = sem("norm_ms_ready")
        norm_rstd_ready = sem("norm_rstd_ready")
        norm_scaled = sem("norm_scaled")
        norm_turned = sem("norm_turned")
        norm_hi_ready = sem("norm_hi_ready")
        norm_lo_ready = sem("norm_lo_ready")
        qk_summed = sem("qk_summed")
        qk_stored = sem("qk_stored")
        v_stored = sem("v_stored")
        qk_squared = sem("qk_squared")
        qk_ss_ready = sem("qk_ss_ready")
        qk_ms_ready = sem("qk_ms_ready")
        qk_rstd_ready = sem("qk_rstd_ready")
        qk_normed = sem("qk_normed")
        qk_turned = sem("qk_turned")
        qkT_stored = sem("qkT_stored")
        scores_done = sem("scores_done")
        scores_biased = sem("scores_biased")
        neg_max_ready = sem("neg_max_ready")
        exps_done = sem("exps_done")
        recip_ready = sem("recip_ready")
        coef_ready = sem("coef_ready")
        second_scaled = sem("second_scaled")
        probs_ready = sem("probs_ready")
        probs_turned = sem("probs_turned")
        probsT_stored = sem("probsT_stored")
        values_summed = sem("values_summed")
        o_squared = sem("o_squared")
        o_ms_ready = sem("o_ms_ready")
        o_rstd_ready = sem("o_rstd_ready")
        o_normed = sem("o_normed")
        o_turned = sem("o_turned")
        oT_stored = sem("oT_stored")
        proj_summed = sem("proj_summed")
        resid_added = sem("resid_added")
        ffn_summed = sem("ffn_summed")
        conv_tap2 = sem("conv_tap2")
        conv_tap1 = sem("conv_tap1")
        conv_done = sem("conv_done")
        gate_ready = sem("gate_ready")
        hidden_ready = sem("hidden_ready")
        out_landed = [sem(f"out_landed{half}") for half in range(2)]

        qkv_rows = w_qkv[0].rearrange("(k p) (s c) -> k p s c", p=P, s=3)
        o_rows = w_o[0].rearrange("(k p) (h c) -> k h p c", p=P, h=2)
        in_rows = w_in[0].rearrange("(k p) (s c) -> k p s c", p=P, s=2)
        out_rows = w_out[0].rearrange("(k p) (h c) -> k h p c", p=P, h=2)
        x_rows = x[0].rearrange("(b p) d -> b p d", p=P)
        result_rows = out[0].rearrange("(b p) d -> b p d", p=P)

        def on_all(vector, n):
            return bass.AP(tensor=vector.tensor, offset=vector.offset, ap=[[0, P], [1, n]])

        def projection_banks(first):
            return [(first + 2 * b + c, b, c) for b in range(NB) for c in range(2)]

        O_FIRST_BANK = (0, 4)
        OUT_FIRST_BANK = (4, 0)

        def store_half(eng, half):
            for i, (_, b, c) in enumerate(projection_banks(0)):
                eng.wait_ge(resid_added, (2 + half) * 2 * NB + i + 1)
                cols = slice(half * HALF + c * BANK, half * HALF + (c + 1) * BANK)
                eng.dma_start(result_rows[b][:, cols], resid[:, b, cols]).then_inc(out_landed[half], 16)

        block = ctx.enter_context(nc.Block())

        @block.sync
        def _(sp):
            def load(n, slot, dst_cols, src, first=False):
                if not first:
                    sp.wait_ge(lo_ready, n - RAW_SLOTS + 1)
                dst = weight_raw[:, slot, 0:dst_cols]
                if len(src.shape) == 3:
                    dst = dst.rearrange("p (s c) -> p s c", s=src.shape[1])
                sp.dma_start(dst, src).then_inc(raw_landed[slot], 16)

            def load_qkv(g, k, first=False):
                load(g * KC + k, k % RAW_SLOTS, 3 * QW, qkv_rows[k][:, :, bass.ds(g * QW, QW)], first)

            for b in range(NB):
                sp.dma_start(resid[:, b, :], x_rows[b]).then_inc(x_landed[b], 16)
            for k in range(KC):
                load_qkv(0, k, first=k < RAW_SLOTS)
            with sp.Fori(1, QKV_GROUPS) as g:
                for k in range(KC):
                    load_qkv(g, k)
            for half in range(2):
                with sp.Fori(0, HEADS // RAW_SLOTS) as i:
                    for j in range(RAW_SLOTS):
                        load(O_BASE + half * HEADS + i * RAW_SLOTS + j, j, SUB,
                             o_rows[bass.ds(i * RAW_SLOTS + j, 1), half, :, :].squeeze(0))
                if half == 1:
                    sp.wait_ge(oT_stored, HEADS)
                    sp.dma_start(gain_all, on_all(ffn_norm_g, D)).then_inc(gain_landed[1], 16)
            with sp.Fori(0, FFN_GROUPS) as g:
                for k in range(KC):
                    load(IN_BASE + g * KC + k, k % RAW_SLOTS, SUB, in_rows[k][:, :, bass.ds(g * BANK, BANK)])
            with sp.Fori(0, FC // RAW_SLOTS) as i:
                for j in range(RAW_SLOTS):
                    load(OUT_BASE + i * RAW_SLOTS + j, j, SUB,
                         out_rows[bass.ds(i * RAW_SLOTS + j, 1), 0, :, :].squeeze(0))
            rest = FC % RAW_SLOTS
            for j in range(rest):
                load(OUT_BASE + FC - rest + j, j, SUB, out_rows[FC - rest + j, 0])
            for j in range(rest):
                load(OUT_BASE + FC + j, rest + j, SUB, out_rows[j, 1])
            with sp.Fori(0, FC // RAW_SLOTS) as i:
                for j in range(RAW_SLOTS):
                    load(OUT_BASE + FC + rest + i * RAW_SLOTS + j, j, SUB,
                         out_rows[bass.ds(i * RAW_SLOTS + j + rest, 1), 1, :, :].squeeze(0))
            store_half(sp, 1)
            for half in range(2):
                sp.wait_ge(out_landed[half], 2 * NB * 16)

        @block.gpsimd
        def _(pool):
            pool.memset(ident[:, :], 0.0).then_inc(ident_zero, 1)
            pool.memset(power[:, :], -0.5).then_inc(power_ready, 1)
            pool.memset(eps[:, :], EPS).then_inc(power_ready, 1)
            pool.memset(bias_rows[:, S:TABLE_W], MASKED).then_inc(mask_ready, 1)
            pool.wait_ge(ident_zero, 1)
            pool.affine_select(out=ident[:, :], in_=ident[:, :], compare_op=ALU.not_equal, fill=1.0, base=0,
                               pattern=[[-1, P]], channel_multiplier=1).then_inc(ident_ready, 1)
            pool.wait_ge(table_stored, 1)
            pool.wait_ge(mask_ready, 1)
            pool.dma_start(bias_scratch, bias_rows).then_inc(bias_written, 16)
            pool.wait_ge(bias_written, 16)
            pool.wait_ge(power_ready, 2)

            def norm_rstd_step(which, b):
                n = which * NB + b + 1
                pool.wait_ge(norm_summed, n)
                pool.tensor_tensor(norm_ms[:, b:b + 1], norm_sum[:, b:b + 1], eps[:, b:b + 1],
                                   ALU.add).then_inc(norm_ms_ready, 1)
                pool.wait_ge(norm_ms_ready, n)
                pool.tensor_tensor(norm_rstd[:, b:b + 1], norm_ms[:, b:b + 1], power[:, b:b + 1],
                                   ALU.pow).then_inc(norm_rstd_ready, 1)

            def attention_rstds(g):
                pool.wait_ge(qk_ss_ready, g + 1)
                pool.tensor_tensor(qk_ms[:, :], qk_ss[:, :], eps[:, :], ALU.add).then_inc(qk_ms_ready, 1)
                pool.wait_ge(qk_ms_ready, g + 1)
                pool.tensor_tensor(qk_rstd[:, :], qk_ms[:, :], power[:, :], ALU.pow).then_inc(qk_rstd_ready, 1)
                for j in range(2):
                    pool.wait_ge(o_squared, 2 * g + j + 1)
                    pool.tensor_tensor(o_ms[:, j, :], o_ss[:, j, :], eps[:, 0:NB],
                                       ALU.add).then_inc(o_ms_ready, 1)
                    pool.wait_ge(o_ms_ready, 2 * g + j + 1)
                    pool.tensor_tensor(o_rstd[:, j, :], o_ms[:, j, :], power[:, 0:NB],
                                       ALU.pow).then_inc(o_rstd_ready, 1)

            for b in range(NB):
                norm_rstd_step(0, b)
            for i in range(BIAS_PARTS):
                n = MAPS // BIAS_PARTS
                pool.dma_start(bass.AP(tensor=bias_copies.tensor, offset=i * n * TABLE_W,
                                       ap=[[MAPS * TABLE_W, P], [TABLE_W, n], [1, TABLE_W]]),
                               bass.AP(tensor=bias_scratch.tensor, offset=i * n * TABLE_W,
                                       ap=[[0, P], [TABLE_W, n], [1, TABLE_W]])).then_inc(bias_copied[i], 16)
            for i in range(BIAS_PARTS):
                n = MAPS // BIAS_PARTS
                pool.wait_ge(bias_copied[i], 16)
                pool.dma_start(pos_bias[:, i * n:(i + 1) * n, :],
                               bass.AP(tensor=bias_copies.tensor, offset=i * n * TABLE_W + P - 1,
                                       ap=[[MAPS * TABLE_W - 1, P], [TABLE_W, n], [1, S]])).then_inc(bias_landed, 16)
            with pool.Fori(0, QKV_GROUPS) as g:
                attention_rstds(g)
            for b in range(NB):
                norm_rstd_step(1, b)
            store_half(pool, 0)

        @block.scalar
        def _(act):
            act.dma_start(table_sb[:, :], rel_table).then_inc(table_landed, 16)
            act.dma_start(onehot_sb, bucket_onehot).then_inc(table_landed, 16)
            act.dma_start(gain_all, on_all(attn_norm_g, D)).then_inc(gain_landed[0], 16)
            for t in range(TAPS):
                act.dma_start(conv_rows[:, t, :], conv_w[0, t].rearrange("(c p) -> c p", p=P)).then_inc(conv_landed, 16)
            act.dma_start(conv_rows[:, TAPS, :], conv_b[0].rearrange("(c p) -> c p", p=P)).then_inc(conv_landed, 16)
            for m in range(2):
                rows = slice(m * HEAD_DIM, (m + 1) * HEAD_DIM)
                act.dma_start(gains[rows, 0:1], q_gain[0].rearrange("(d a) -> d a", a=1)).then_inc(small_landed, 16)
                act.dma_start(gains[rows, 1:2], k_gain[0].rearrange("(d a) -> d a", a=1)).then_inc(small_landed, 16)
            act.dma_start(gains[:, 3:4], sub_gain[0].rearrange("(d a) -> d a", a=1)).then_inc(small_landed, 16)
            for i, vec in enumerate((lam_q1, lam_k1, lam_q2, lam_k2)):
                act.dma_start(lam_vecs[:, i, :], on_all(vec, HEAD_DIM)).then_inc(small_landed, 16)

            def split_weights(n, slot, cols):
                act.wait_ge(raw_landed[slot % RAW_SLOTS], (n - slot % RAW_SLOTS) * (16 // RAW_SLOTS) + 16)
                if not (isinstance(n, int) and n < SPLIT_SLOTS):
                    act.wait_ge(weights_used, n - SPLIT_SLOTS + 1)
                act.activation(weight_hi[:, slot % SPLIT_SLOTS, 0:cols], weight_raw[:, slot % RAW_SLOTS, 0:cols],
                               ACT.Copy).then_inc(hi_ready, 1)

            def split_chunk(slot, src):
                act.activation(chunk_hi[:, slot % SPLIT_SLOTS, :], src, ACT.Copy).then_inc(chunk_hi_ready, 1)

            def norm_squares(n, b, piece, cols):
                if n:
                    act.wait_ge(norm_squared, n)
                act.activation(norm_junk[:, 0:cols.stop - cols.start], resid[:, b, cols], ACT.Square, scale=D ** -0.5,
                               accum_out=norm_sq[:, b, piece:piece + 1]).then_inc(norm_squared, 1)

            def norm_hi(which, b, i):
                n = (which * NB + b) * PIECES + i + 1
                act.wait_ge(norm_turned, n)
                act.activation(act_hi[:, 4 * i:4 * i + 4, b * P:(b + 1) * P],
                               psum[:, 4 * b + i, :].rearrange("p (c t) -> p c t", t=P),
                               ACT.Copy).then_inc(norm_hi_ready, 1)

            def attention(g, step):
                def turned(j):
                    act.wait_ge(qk_turned, 2 * g + j + 1)
                    act.activation(qT[:, j, :], ps_qkT[:, 0:S], ACT.Copy, scale=gains[:, 2:3])
                    act.activation(kT[:, j, :], ps_qkT[:, S:2 * S], ACT.Copy).then_inc(qkT_stored, 1)

                def exps(j):
                    act.wait_ge(neg_max_ready, 2 * g + j + 1)
                    for m in range(2):
                        act.activation(scores1[:, j, m, :], scores1[:, j, m, :], ACT.Exp,
                                       bias=neg_max[:, j, 2 + m:3 + m], accum_out=exp_sum[:, j, 2 + m:3 + m])
                    for m in range(2):
                        ins = act.activation(scores0[:, j, m, :], scores0[:, j, m, :], ACT.Exp,
                                             bias=neg_max[:, j, m:m + 1], accum_out=exp_sum[:, j, m:m + 1])
                    ins.then_inc(exps_done, 1)

                def store_probsT(j):
                    act.wait_ge(probs_turned, 2 * g + j + 1)
                    act.activation(probsT[:, j, :, :], ps_pT, ACT.Copy).then_inc(probsT_stored, 1)

                def square_o(j):
                    act.wait_ge(values_summed, 2 * g + j + 1)
                    act.wait_ge(o_squared, 2 * g + j)
                    for b in range(NB):
                        ins = act.activation(o_junk[:, b * VD:(b + 1) * VD], ps_o[:, b, :], ACT.Square, scale=VD ** -0.5,
                                             accum_out=o_ss[:, j, b:b + 1])
                    ins.then_inc(o_squared, 1)

                def store_oT(j):
                    act.wait_ge(o_turned, 2 * g + j + 1)
                    act.activation(attn_out[:, bass.ds(2 * g + j, 1), :].squeeze(1), ps_oT, ACT.Copy,
                                   scale=gains[:, 4:5]).then_inc(oT_stored, 1)

                if step == 2:
                    for b in range(NB):
                        act.wait_ge(qk_summed, NB * g + b + 1)
                        act.activation(qk[:, b, :], psum[:, b, :], ACT.Copy).then_inc(qk_stored, 1)
                    act.wait_ge(qk_stored, NB * g + NB)
                    act.activation(qk_sq, qk.rearrange("p b c -> p (b c)"), ACT.Square,
                                   scale=HEAD_DIM ** -0.5).then_inc(qk_squared, 1)
                if step == 5:
                    turned(0)
                if step == 7:
                    turned(1)
                    exps(0)
                if step == 9:
                    store_probsT(0)
                    exps(1)
                if step == 10:
                    square_o(0)
                if step == 11:
                    store_probsT(1)
                if step == 12:
                    store_oT(0)
                    square_o(1)
                if step == 14:
                    store_oT(1)

            def convolve(g, bank, first_bank):
                if bank < 3:
                    act.wait_ge(ffn_summed, 3 * g + bank + 1)
                else:
                    act.wait_ge(weights_used, IN_BASE + (g + 1) * KC)
                for u in range(2):
                    i = 2 * bank + u
                    col = (FC if i >= FFN_BLOCKS else 0) + g * FFN_BLOCKS + i % FFN_BLOCKS
                    dst = (pre_gate if i < FFN_BLOCKS else pre_up)[:, i % FFN_BLOCKS, :]
                    ins = act.activation(dst, psum[:, first_bank + bank, u * S:(u + 1) * S], ACT.Identity,
                                         bias=conv_cols[:, TAPS, bass.ds(col, 1)],
                                         scale=conv_cols[:, TAPS - 1, bass.ds(col, 1)])
                ins.then_inc(conv_tap2, 1)

            def hidden_step(g, step, first_bank):
                if 2 <= step < 6:
                    if step == 2 and not (isinstance(g, int) and g == 0):
                        act.wait_ge(hidden_ready, g)
                    convolve(g, step - 2, first_bank)
                if step == 6:
                    act.wait_ge(conv_done, 4 * g + 2)
                    act.activation(pre_gate, pre_gate, ACT.Silu).then_inc(gate_ready, 1)

            act.wait_ge(conv_turned, 1)
            act.activation(conv_cols[:, :, :], psum[:, 7, 0:(TAPS + 1) * 2 * FC].rearrange("p (t c) -> p t c", c=2 * FC),
                           ACT.Copy).then_inc(conv_stored, 1)
            act.wait_ge(x_landed[0], 16)
            for i in range(2):
                norm_squares(i, 0, i, slice(i * HALF, (i + 1) * HALF))
            act.wait_ge(x_landed[1], 16)
            for i in range(2):
                norm_squares(2 + i, 1, i, slice(i * HALF, (i + 1) * HALF))
            act.wait_ge(lam_step, 2)
            act.activation(lam_exp[:, :], lam_dot[:, :], ACT.Exp).then_inc(lam_exped, 1)
            for n in range(2):
                split_weights(n, n, 3 * QW)
            for b in range(NB):
                for i in range(PIECES):
                    norm_hi(0, b, i)
            for k in range(2, KC):
                split_weights(k, k, 3 * QW)
            act.wait_ge(bias_landed, BIAS_PARTS * 16)
            with act.Fori(1, QKV_GROUPS) as g:
                for k in range(KC):
                    split_weights(g * KC + k, k, 3 * QW)
                    attention(g - 1, k)
            for h in range(HEADS):
                split_weights(O_BASE + h, h, SUB)
                if h >= HEADS - 2:
                    act.wait_ge(oT_stored, h + 1)
                split_chunk(h, attn_out[:, h, :])
                attention(QKV_GROUPS - 1, h)
            for h in range(HEADS):
                split_weights(O_BASE + HEADS + h, h, SUB)
                split_chunk(h, attn_out[:, h, :])
                if 4 <= h < 4 + 2 * NB:
                    i = h - 4
                    act.wait_ge(resid_added, i + 1)
                    norm_squares(4 + i, i // 2, i % 2, slice((i % 2) * BANK, (i % 2 + 1) * BANK))
            for n in range(3):
                split_weights(IN_BASE + n, n, SUB)
            for i in range(2 * NB):
                act.wait_ge(resid_added, 2 * NB + i + 1)
                norm_squares(8 + i, i // 2, 2 + i % 2, slice(HALF + (i % 2) * BANK, HALF + (i % 2 + 1) * BANK))
            for b in range(NB):
                for i in range(PIECES):
                    norm_hi(1, b, i)
            for k in range(3, KC):
                split_weights(IN_BASE + k, k, SUB)
            with act.Fori(0, FFN_GROUPS // 2) as pair:
                for odd in range(2):
                    for k in range(KC):
                        split_weights(IN_BASE + (pair * 2 + odd + 1) * KC + k, k, SUB)
                        hidden_step(pair * 2 + odd, k, 4 * odd)
            for j in range(RAW_SLOTS):
                split_weights(OUT_BASE + j, j, SUB)
                split_chunk(j, hidden[:, j, :])
                hidden_step(FFN_GROUPS - 1, j, 0)
            with act.Fori(1, FC // RAW_SLOTS) as i:
                for j in range(RAW_SLOTS):
                    split_weights(OUT_BASE + i * RAW_SLOTS + j, j, SUB)
                    split_chunk(j, hidden[:, bass.ds(i * RAW_SLOTS + j, 1), :].squeeze(1))
            rest = FC % RAW_SLOTS
            for j in range(rest):
                split_weights(OUT_BASE + FC - rest + j, j, SUB)
                if j == 0:
                    act.wait_ge(hidden_ready, FFN_GROUPS)
                split_chunk(j, hidden[:, FC - rest + j, :])
            for j in range(rest):
                split_weights(OUT_BASE + FC + j, rest + j, SUB)
                split_chunk(rest + j, hidden[:, j, :])
            with act.Fori(0, FC // RAW_SLOTS) as i:
                for j in range(RAW_SLOTS):
                    split_weights(OUT_BASE + FC + rest + i * RAW_SLOTS + j, j, SUB)
                    split_chunk(j, hidden[:, bass.ds(i * RAW_SLOTS + j + rest, 1), :].squeeze(1))

        @block.vector
        def _(dve):
            def split_weights(n, slot, cols):
                dve.wait_ge(hi_ready, n + 1)
                dve.tensor_tensor(weight_lo[:, slot % SPLIT_SLOTS, 0:cols], weight_raw[:, slot % RAW_SLOTS, 0:cols],
                                  weight_hi[:, slot % SPLIT_SLOTS, 0:cols].bitcast(F32),
                                  ALU.subtract).then_inc(lo_ready, 1)

            def split_chunk(m, slot, src):
                dve.wait_ge(chunk_hi_ready, m + 1)
                dve.tensor_tensor(chunk_lo[:, slot % SPLIT_SLOTS, :], src,
                                  chunk_hi[:, slot % SPLIT_SLOTS, :].bitcast(F32),
                                  ALU.subtract).then_inc(chunk_lo_ready, 1)

            def norm_total(which, b, pieces):
                dve.wait_ge(norm_squared, 2 * NB + 2 * NB + 2 * (b + 1) if which else 2 * (b + 1))
                dve.tensor_reduce(norm_sum[:, b:b + 1], norm_sq[:, b, 0:pieces], AX_X, ALU.add).then_inc(norm_summed, 1)

            def normalise(which):
                dve.wait_ge(gain_landed[which], 16)
                for b in range(NB):
                    dve.wait_ge(norm_rstd_ready, which * NB + b + 1)
                    first = (which * NB + b) * PIECES
                    for i in range(PIECES):
                        if b:
                            dve.wait_ge(norm_turned, first - PIECES + i + 1)
                        cols = slice(i * BANK, (i + 1) * BANK)
                        dve.scalar_tensor_tensor(out=scaled[:, cols], in0=resid[:, b, cols],
                                                 scalar=norm_rstd[:, b:b + 1], in1=gain_all[:, cols],
                                                 op0=ALU.mult, op1=ALU.mult).then_inc(norm_scaled, 1)
                    for i in range(PIECES):
                        dve.wait_ge(norm_hi_ready, first + i + 1)
                        tokens = slice(b * P, (b + 1) * P)
                        dve.tensor_tensor(act_lo[:, 4 * i:4 * i + 4, tokens],
                                          psum[:, 4 * b + i, :].rearrange("p (c t) -> p c t", t=P),
                                          act_hi[:, 4 * i:4 * i + 4, tokens].bitcast(F32),
                                          ALU.subtract).then_inc(norm_lo_ready, 1)

            def attention(g, step):
                def bias(j):
                    n = 2 * g + j + 1
                    dve.wait_ge(scores_done, n)
                    maps = bass.ds(4 * g + 2 * j, 2)
                    dve.tensor_tensor(scores1[:, j, :, :], ps_s1, pos_bias[:, maps, :], ALU.add)
                    dve.tensor_tensor(scores0[:, j, :, :], ps_s0, pos_bias[:, maps, P:S],
                                      ALU.add).then_inc(scores_biased, 1)
                    dve.wait_ge(scores_biased, n)
                    dve.tensor_reduce(neg_max[:, j, 2:4], scores1[:, j, :, :], AX_X, ALU.max, negate=True)
                    dve.tensor_reduce(neg_max[:, j, 0:2], scores0[:, j, :, :], AX_X, ALU.max,
                                      negate=True).then_inc(neg_max_ready, 1)

                def combine(j):
                    n = 2 * g + j + 1
                    dve.wait_ge(exps_done, n)
                    dve.reciprocal(coef[:, j, :], exp_sum[:, j, :]).then_inc(recip_ready, 1)
                    dve.wait_ge(recip_ready, n)
                    second = coef[:, j, :].rearrange("p (b m) -> p b m", m=2)[:, :, 1]
                    dve.tensor_scalar(second, second, neg_lam[:, :], None, ALU.mult).then_inc(coef_ready, 1)
                    dve.wait_ge(coef_ready, n)
                    dve.tensor_scalar(scores1[:, j, 1, :], scores1[:, j, 1, :], coef[:, j, 3:4], None, ALU.mult)
                    dve.tensor_scalar(scores0[:, j, 1, :], scores0[:, j, 1, :], coef[:, j, 1:2], None,
                                      ALU.mult).then_inc(second_scaled, 1)
                    dve.wait_ge(second_scaled, n)
                    dve.scalar_tensor_tensor(out=scores1[:, j, 0, :], in0=scores1[:, j, 0, :],
                                             scalar=coef[:, j, 2:3], in1=scores1[:, j, 1, :],
                                             op0=ALU.mult, op1=ALU.add)
                    dve.scalar_tensor_tensor(out=scores0[:, j, 0, :], in0=scores0[:, j, 0, :],
                                             scalar=coef[:, j, 0:1], in1=scores0[:, j, 1, :],
                                             op0=ALU.mult, op1=ALU.add).then_inc(probs_ready, 1)

                def norm_o(j):
                    dve.wait_ge(o_rstd_ready, 2 * g + j + 1)
                    dve.tensor_tensor(head_out[:, j, :, :], ps_o,
                                      o_rstd[:, j, :].unsqueeze(2).to_broadcast([P, NB, VD]),
                                      ALU.mult).then_inc(o_normed, 1)

                if step == 2:
                    dve.wait_ge(weights_used, (g + 1) * KC)
                    dve.tensor_copy(v_sb, psum[:, NB, :].rearrange("p (b c) -> p b c", b=NB)).then_inc(v_stored, 1)
                if step == 3:
                    dve.wait_ge(qk_squared, g + 1)
                    dve.tensor_reduce(qk_ss[:, :], qk_sq.rearrange("p (m d) -> p m d", d=HEAD_DIM), AX_X,
                                      ALU.add).then_inc(qk_ss_ready, 1)
                if step == 4:
                    dve.wait_ge(qk_rstd_ready, g + 1)
                    rows = qk.rearrange("p b (m d) -> p (b m) d", d=HEAD_DIM)
                    dve.tensor_tensor(rows, rows, qk_rstd[:, :].unsqueeze(2).to_broadcast([P, GROUP_RSTD, HEAD_DIM]),
                                      ALU.mult).then_inc(qk_normed, 1)
                if step == 6:
                    bias(0)
                if step == 8:
                    combine(0)
                    bias(1)
                if step == 10:
                    combine(1)
                if step == 11:
                    norm_o(0)
                if step == 13:
                    norm_o(1)

            def convolve(g, bank, first_bank):
                n = 4 * g + bank + 1
                dve.wait_ge(conv_tap2, n)
                for tap in range(TAPS - 2, -1, -1):
                    shift = TAPS - 1 - tap
                    for u in range(2):
                        i = 2 * bank + u
                        col = (FC if i >= FFN_BLOCKS else 0) + g * FFN_BLOCKS + i % FFN_BLOCKS
                        dst = (pre_gate if i < FFN_BLOCKS else pre_up)[:, i % FFN_BLOCKS, shift:S]
                        ins = dve.scalar_tensor_tensor(
                            out=dst, in0=psum[:, first_bank + bank, u * S:(u + 1) * S - shift],
                            scalar=conv_cols[:, tap, bass.ds(col, 1)], in1=dst, op0=ALU.mult, op1=ALU.add)
                    ins.then_inc(conv_done if tap == 0 else conv_tap1, 1)
                    if tap:
                        dve.wait_ge(conv_tap1, n)

            def hidden_step(g, step, first_bank, steps):
                if step in steps[0:4]:
                    convolve(g, steps.index(step), first_bank)
                if step == steps[4]:
                    dve.wait_ge(gate_ready, g + 1)
                    dve.wait_ge(conv_done, 4 * g + 4)
                    dve.tensor_tensor(hidden[:, bass.ds(g * FFN_BLOCKS, FFN_BLOCKS), :], pre_gate, pre_up,
                                      ALU.mult).then_inc(hidden_ready, 1)

            def add_residual(half, i, first_bank, stage, used):
                bank, b, c = projection_banks(first_bank)[i]
                cols = slice(half * HALF + c * BANK, half * HALF + (c + 1) * BANK)
                if i < 2 * NB - 1:
                    dve.wait_ge(proj_summed, (2 * stage + half) * (2 * NB - 1) + i + 1)
                else:
                    dve.wait_ge(weights_used, used)
                dve.tensor_tensor(resid[:, b, cols], psum[:, bank, :], resid[:, b, cols],
                                  ALU.add).then_inc(resid_added, 1)

            dve.wait_ge(table_summed, 1)
            dve.tensor_copy(bias_rows[:, 0:S], psum[0:MAPS, 6, 0:S]).then_inc(table_stored, 1)
            for b in range(NB):
                norm_total(0, b, 2)
            dve.wait_ge(small_landed, 9 * 16)
            dve.tensor_tensor(gains[:, 2:3], gains[:, 0:1], gains[:, 1:2], ALU.mult).then_inc(gains_step, 1)
            dve.tensor_scalar(gains[:, 4:5], gains[:, 3:4], 1.0 - LAM_INIT, None, ALU.mult).then_inc(gains_step, 1)
            lam_pairs = lam_vecs[:, :, :].rearrange("p (i s) d -> p i s d", s=2)
            dve.tensor_tensor(lam_prod[:, :, :], lam_pairs[:, :, 0, :], lam_pairs[:, :, 1, :],
                              ALU.mult).then_inc(lam_step, 1)
            dve.wait_ge(gains_step, 2)
            dve.tensor_scalar(gains[:, 2:3], gains[:, 2:3], HEAD_DIM ** -0.5, None, ALU.mult).then_inc(gains_step, 1)
            dve.wait_ge(lam_step, 1)
            dve.tensor_reduce(lam_dot[:, :], lam_prod[:, :, :], AX_X, ALU.add).then_inc(lam_step, 1)
            normalise(0)
            dve.wait_ge(lam_exped, 1)
            dve.tensor_tensor(lam_diff[:, :], lam_exp[:, 1:2], lam_exp[:, 0:1], ALU.subtract).then_inc(lam_step, 1)
            dve.wait_ge(lam_step, 3)
            dve.tensor_scalar(neg_lam[:, :], lam_diff[:, :], LAM_INIT, None, ALU.subtract).then_inc(lam_step, 1)
            for k in range(KC):
                split_weights(k, k, 3 * QW)
            dve.wait_ge(lam_step, 4)
            dve.wait_ge(bias_landed, BIAS_PARTS * 16)
            with dve.Fori(1, QKV_GROUPS) as g:
                for k in range(KC):
                    split_weights(g * KC + k, k, 3 * QW)
                    attention(g - 1, k)
            for h in range(HEADS):
                split_weights(O_BASE + h, h, SUB)
                split_chunk(h, h, attn_out[:, h, :])
                attention(QKV_GROUPS - 1, h)
            for h in range(HEADS):
                split_weights(O_BASE + HEADS + h, h, SUB)
                split_chunk(HEADS + h, h, attn_out[:, h, :])
                if 3 <= h < 3 + 2 * NB:
                    add_residual(0, h - 3, O_FIRST_BANK[0], 0, O_BASE + HEADS)
            for n in range(3):
                split_weights(IN_BASE + n, n, SUB)
            for i in range(2 * NB):
                add_residual(1, i, O_FIRST_BANK[1], 0, IN_BASE)
            for b in range(NB):
                norm_total(1, b, 4)
            normalise(1)
            for k in range(3, KC):
                split_weights(IN_BASE + k, k, SUB)
            with dve.Fori(0, FFN_GROUPS // 2) as pair:
                for odd in range(2):
                    for k in range(KC):
                        split_weights(IN_BASE + (pair * 2 + odd + 1) * KC + k, k, SUB)
                        hidden_step(pair * 2 + odd, k, 4 * odd, (3, 5, 7, 9, 10))
            for j in range(RAW_SLOTS):
                split_weights(OUT_BASE + j, j, SUB)
                split_chunk(2 * HEADS + j, j, hidden[:, j, :])
                hidden_step(FFN_GROUPS - 1, j, 0, (3, 4, 5, 6, 7))
            with dve.Fori(1, FC // RAW_SLOTS) as i:
                for j in range(RAW_SLOTS):
                    split_weights(OUT_BASE + i * RAW_SLOTS + j, j, SUB)
                    split_chunk(2 * HEADS + i * RAW_SLOTS + j, j, hidden[:, bass.ds(i * RAW_SLOTS + j, 1), :].squeeze(1))
            rest = FC % RAW_SLOTS
            for j in range(rest):
                split_weights(OUT_BASE + FC - rest + j, j, SUB)
                split_chunk(2 * HEADS + FC - rest + j, j, hidden[:, FC - rest + j, :])
            for j in range(rest):
                split_weights(OUT_BASE + FC + j, rest + j, SUB)
                split_chunk(2 * HEADS + FC + j, rest + j, hidden[:, j, :])
                if j >= rest - 2:
                    for i in range(NB):
                        add_residual(0, NB * (j - rest + 2) + i, OUT_FIRST_BANK[0], 1, OUT_BASE + FC)
            with dve.Fori(0, FC // RAW_SLOTS) as i:
                for j in range(RAW_SLOTS):
                    split_weights(OUT_BASE + FC + rest + i * RAW_SLOTS + j, j, SUB)
                    split_chunk(2 * HEADS + FC + rest + i * RAW_SLOTS + j, j,
                                hidden[:, bass.ds(i * RAW_SLOTS + j + rest, 1), :].squeeze(1))
            for i in range(2 * NB):
                add_residual(1, i, OUT_FIRST_BANK[1], 1, OUT_BASE + 2 * FC)

        @block.tensor
        def _(pe):
            def product(dst, left, right, start, stop):
                (left_hi, left_lo), (right_hi, right_lo) = left, right
                pe.matmul(dst, left_hi, right_hi, start=start, stop=False, skip_group_check=True)
                pe.matmul(dst, left_hi, right_lo, start=False, stop=False, skip_group_check=True)
                return pe.matmul(dst, left_lo, right_hi, start=False, stop=stop, skip_group_check=True)

            def act_part(k, tokens):
                return act_hi[:, k, tokens], act_lo[:, k, tokens]

            def weight_part(slot, cols):
                return weight_hi[:, slot % SPLIT_SLOTS, cols], weight_lo[:, slot % SPLIT_SLOTS, cols]

            def qkv(g, k, first=False):
                pe.wait_ge(lo_ready, g * KC + k + 1)
                for b in range(NB):
                    if k == 0 and not first:
                        pe.wait_ge(qk_stored, NB * (g - 1) + b + 1)
                    mm = product(psum[:, b, :], act_part(k, slice(b * P, (b + 1) * P)),
                                 weight_part(k, slice(0, 2 * QW)), k == 0, k == KC - 1)
                    if k == KC - 1:
                        mm.then_inc(qk_summed, 1)
                if k == 0 and not first:
                    pe.wait_ge(v_stored, g)
                for b in range(NB):
                    mm = product(psum[:, NB, b * QW:(b + 1) * QW], act_part(k, slice(b * P, (b + 1) * P)),
                                 weight_part(k, slice(2 * QW, 3 * QW)), k == 0 and b == 0, k == KC - 1)
                mm.then_inc(weights_used, 1)

            def turn(dst, src, k=P):
                return pe.transpose(dst, src, ident[0:k, 0:k])

            def attention(g, step):
                def turn_qk(j):
                    pe.wait_ge(qk_normed, g + 1)
                    if j == 1:
                        pe.wait_ge(qkT_stored, 2 * g + 1)
                    for part in range(2):
                        for b in range(NB):
                            cols = slice(part * QW + j * VD, part * QW + (j + 1) * VD)
                            mm = turn(ps_qkT[:, part * S + b * P:part * S + (b + 1) * P], qk[:, b, cols])
                    mm.then_inc(qk_turned, 1)

                def score(j):
                    pe.wait_ge(qkT_stored, 2 * g + j + 1)
                    if j == 1:
                        pe.wait_ge(scores_biased, 2 * g + 1)
                    for m in range(2):
                        rows = slice(m * HEAD_DIM, (m + 1) * HEAD_DIM)
                        pe.matmul(ps_s1[:, m, :], qT[rows, j, P:S], kT[rows, j, :], start=True, stop=True)
                    for m in range(2):
                        rows = slice(m * HEAD_DIM, (m + 1) * HEAD_DIM)
                        mm = pe.matmul(ps_s0[:, m, :], qT[rows, j, 0:P], kT[rows, j, 0:P], start=True, stop=True)
                    mm.then_inc(scores_done, 1)

                def turn_probs(j):
                    pe.wait_ge(probs_ready, 2 * g + j + 1)
                    if j == 1:
                        pe.wait_ge(probsT_stored, 2 * g + 1)
                    for c in range(NB):
                        turn(ps_pT[:, c, :], scores1[:, j, 0, c * P:(c + 1) * P])
                    turn(ps_pT[:, NB, :], scores0[:, j, 0, :]).then_inc(probs_turned, 1)

                def values(j):
                    pe.wait_ge(probsT_stored, 2 * g + j + 1)
                    if j == 0:
                        pe.wait_ge(qkT_stored, 2 * g + 2)
                    else:
                        pe.wait_ge(o_normed, 2 * g + 1)
                    cols = slice(j * VD, (j + 1) * VD)
                    pe.matmul(ps_o[:, 0, :], probsT[:, j, NB, :], v_sb[:, 0, cols], start=True, stop=True)
                    pe.matmul(ps_o[:, 1, :], probsT[:, j, 0, :], v_sb[:, 0, cols], start=True, stop=False)
                    pe.matmul(ps_o[:, 1, :], probsT[:, j, 1, :], v_sb[:, 1, cols], start=False,
                              stop=True).then_inc(values_summed, 1)

                def turn_o(j):
                    pe.wait_ge(o_normed, 2 * g + j + 1)
                    if j == 0:
                        pe.wait_ge(probsT_stored, 2 * g + 2)
                    else:
                        pe.wait_ge(oT_stored, 2 * g + 1)
                    turn(ps_oT[:, 0:P], head_out[:, j, 0, :])
                    turn(ps_oT[:, P:S], head_out[:, j, 1, :]).then_inc(o_turned, 1)

                if step == 2:
                    if not (isinstance(g, int) and g == 0):
                        pe.wait_ge(oT_stored, 2 * g)
                    turn_qk(0)
                if step == 3:
                    score(0)
                if step == 4:
                    turn_qk(1)
                if step == 5:
                    score(1)
                if step == 6:
                    turn_probs(0)
                if step == 7:
                    values(0)
                if step == 8:
                    turn_probs(1)
                if step == 9:
                    values(1)
                    turn_o(0)
                if step == 11:
                    turn_o(1)

            def project(n, m, slot, banks, start=False, stop=False, free=None):
                pe.wait_ge(lo_ready, n + 1)
                pe.wait_ge(chunk_lo_ready, m + 1)
                for i, (bank, b, c) in enumerate(banks):
                    if start and free:
                        free(i)
                    tokens = slice(b * P, (b + 1) * P)
                    s = slot % SPLIT_SLOTS
                    mm = product(psum[:, bank, :], (chunk_hi[:, s, tokens], chunk_lo[:, s, tokens]),
                                 weight_part(slot, slice(c * BANK, (c + 1) * BANK)), start, stop)
                    if stop and i < 2 * NB - 1:
                        mm.then_inc(proj_summed, 1)
                mm.then_inc(weights_used, 1)

            def ffn_in(g, k, first_bank, free=None):
                pe.wait_ge(lo_ready, IN_BASE + g * KC + k + 1)
                for i in range(2 * FFN_BLOCKS):
                    if k == 0 and i % 2 == 0 and free:
                        free(i // 2)
                    mm = product(psum[:, first_bank + i // 2, (i % 2) * S:(i % 2 + 1) * S],
                                 weight_part(k, slice(i * P, (i + 1) * P)), act_part(k, slice(0, S)),
                                 k == 0 and i % 2 == 0, k == KC - 1)
                    if k == KC - 1 and i % 2 and i < 2 * FFN_BLOCKS - 1:
                        mm.then_inc(ffn_summed, 1)
                mm.then_inc(weights_used, 1)

            pe.wait_ge(table_landed, 32)
            pe.matmul(psum[0:MAPS, 6, 0:S], table_sb[:, :], onehot_sb, start=True,
                      stop=True).then_inc(table_summed, 1)
            pe.wait_ge(ident_ready, 1)
            pe.wait_ge(conv_landed, (TAPS + 1) * 16)
            for t in range(TAPS + 1):
                mm = turn(psum[:, 7, t * 2 * FC:(t + 1) * 2 * FC], conv_rows[:, t, :], 2 * FC)
            mm.then_inc(conv_turned, 1)

            def norm_turn(which):
                for b in range(NB):
                    for i in range(PIECES):
                        pe.wait_ge(norm_scaled, (which * NB + b) * PIECES + i + 1)
                        if which == 0 and b == 1 and i == 2:
                            pe.wait_ge(table_stored, 1)
                        if which == 0 and b == 1 and i == 3:
                            pe.wait_ge(conv_stored, 1)
                        for c in range(4):
                            cols = slice((4 * i + c) * P, (4 * i + c + 1) * P)
                            mm = turn(psum[:, 4 * b + i, c * P:(c + 1) * P], scaled[:, cols])
                        mm.then_inc(norm_turned, 1)

            norm_turn(0)
            for k in range(KC):
                if k % 4 == 0:
                    pe.wait_ge(norm_lo_ready, PIECES + k // 4 + 1)
                qkv(0, k, first=True)
            with pe.Fori(1, QKV_GROUPS) as g:
                for k in range(KC):
                    qkv(g, k)
                    attention(g - 1, k)
            def o_half(half, step):
                n = half * HEADS + step

                def free(i):
                    if half == 1:
                        pe.wait_ge(oT_stored, HEADS)
                    elif i < NB:
                        pe.wait_ge(qk_stored, NB * QKV_GROUPS - NB + i + 1)
                    elif i == NB:
                        pe.wait_ge(v_stored, QKV_GROUPS)

                project(O_BASE + n, n, step, projection_banks(O_FIRST_BANK[half]), step == 0,
                        step == HEADS - 1, free)

            for h in range(HEADS):
                o_half(0, h)
                attention(QKV_GROUPS - 1, h)
            for h in range(HEADS):
                o_half(1, h)
            norm_turn(1)
            for k in range(KC):
                if k % 4 == 0:
                    pe.wait_ge(norm_lo_ready, 3 * PIECES + k // 4 + 1)
                ffn_in(0, k, 0)
            with pe.Fori(0, FFN_GROUPS // 2) as pair:
                for odd in range(2):
                    g = pair * 2 + odd + 1

                    def free(bank):
                        if bank == 0:
                            pe.wait_ge(hidden_ready, g - 1)

                    for k in range(KC):
                        ffn_in(g, k, 4 * (1 - odd), free)
            def out_chunk(half, c, slot, start=False, stop=False):
                def free(i):
                    pe.wait_ge(conv_done, 4 * (FFN_GROUPS - 1 + half))

                project(OUT_BASE + half * FC + c, 2 * HEADS + half * FC + c, slot,
                        projection_banks(OUT_FIRST_BANK[half]), start, stop, free)

            rest = FC % RAW_SLOTS
            for j in range(RAW_SLOTS):
                out_chunk(0, j, j, start=j == 0)
            with pe.Fori(1, FC // RAW_SLOTS) as i:
                for j in range(RAW_SLOTS):
                    out_chunk(0, i * RAW_SLOTS + j, j)
            for j in range(rest):
                out_chunk(0, FC - rest + j, j, stop=j == rest - 1)
            for j in range(rest):
                out_chunk(1, j, rest + j, start=j == 0)
            with pe.Fori(0, FC // RAW_SLOTS - 1) as i:
                for j in range(RAW_SLOTS):
                    out_chunk(1, i * RAW_SLOTS + rest + j, j)
            for j in range(RAW_SLOTS):
                out_chunk(1, FC - RAW_SLOTS + j, j, stop=j == RAW_SLOTS - 1)


INPUTS = ["x", "rel_table", "attn_norm_g", "ffn_norm_g", "da_w_qkv", "da_w_o", "da_q_gain", "da_k_gain",
          "da_lam_q1", "da_lam_k1", "da_lam_q2", "da_lam_k2", "da_sub_gain", "ffn_w_in", "ffn_conv_w",
          "ffn_conv_b", "ffn_w_out"]


def bucket_rows(seq, buckets, max_distance=128):
    import numpy as np

    exact = buckets // 2
    d = np.arange(seq - 1, -1, -1)
    ratio = np.log(np.maximum(d, 1).astype(np.float32) / np.float32(exact)) / np.float32(np.log(max_distance / exact))
    large = np.minimum(exact + (ratio * np.float32(buckets - exact)).astype(np.int32), buckets - 1)
    bucket = np.where(d < exact, d, large)
    return (bucket[None, :] == np.arange(buckets)[:, None]).astype(np.float32)


def kernel(**inputs):
    import numpy as np
    import concourse.bacc as bacc
    from concourse import mybir
    from concourse.bass_utils import run_bass_kernel_spmd

    nc = bacc.Bacc("TRN2", target_bir_lowering=False, num_devices=1)
    arrays = {name: np.ascontiguousarray(inputs[name]) for name in INPUTS}
    arrays["bucket_onehot"] = bucket_rows(inputs["x"].shape[1], inputs["rel_table"].shape[0])
    aps = {name: nc.dram_tensor("in_" + name, a.shape, mybir.dt.from_np(a.dtype), kind="ExternalInput").ap()
           for name, a in arrays.items()}
    out = nc.dram_tensor("result", inputs["x"].shape, mybir.dt.float32, kind="ExternalOutput").ap()
    build_layer(nc, aps["x"], aps["rel_table"], aps["bucket_onehot"], aps["attn_norm_g"], aps["ffn_norm_g"],
                aps["da_w_qkv"], aps["da_w_o"], aps["da_q_gain"], aps["da_k_gain"], aps["da_lam_q1"],
                aps["da_lam_k1"], aps["da_lam_q2"], aps["da_lam_k2"], aps["da_sub_gain"], aps["ffn_w_in"],
                aps["ffn_conv_w"], aps["ffn_conv_b"], aps["ffn_w_out"], out)
    r = run_bass_kernel_spmd(nc, [{"in_" + name: a for name, a in arrays.items()}], core_ids=[0])
    return r.results[0]["result"]
```

```python
from contextlib import ExitStack

import concourse.bass as bass
from concourse import mybir

F32 = mybir.dt.float32
F32R = mybir.dt.float32r
ALU = mybir.AluOpType
ACT = mybir.ActivationFunctionType
AX_X = mybir.AxisListType.X

P = 128
HEAD_DIM = 64
EPS = 1e-6
MASKED = -1e30
LAM_INIT = 0.2
BANK = 512
RAW_SLOTS = 8
SPLIT_SLOTS = 4
SUB = 1024

PE_PARTS = ("turn_qk", "score", "turn_probs", "values", "turn_o")
ACT_PARTS = ("store_qk", "store_qkT", "exps", "store_probsT", "square_o", "store_oT")
DVE_PARTS = ("store_v", "sum_qk", "norm_qk", "bias", "combine", "norm_o")
QKV_PLAN = dict(turn_qk=(4, 5), score=(5, 6), turn_probs=(9, 10), values=(10, 11), turn_o=(12, 13),
                store_qk=(2,), store_qkT=(7, 8), exps=(9, 10), store_probsT=(12, 13), square_o=(13, 14),
                store_oT=(15, 15),
                store_v=(2,), sum_qk=(3,), norm_qk=(5,), bias=(8, 9), combine=(10, 11), norm_o=(13, 14))
O_PLAN = dict(turn_qk=(3, 4), score=(4, 5), turn_probs=(7, 8), values=(8, 9), turn_o=(9, 11),
              store_qk=(2,), store_qkT=(6, 7), exps=(8, 9), store_probsT=(10, 11), square_o=(11, 12),
              store_oT=(12, 14),
              store_v=(2,), sum_qk=(3,), norm_qk=(5,), bias=(7, 8), combine=(9, 10), norm_o=(12, 13))


def run_plan(plan, parts, step, functions):
    for j in range(2):
        for part in parts:
            if j < len(plan[part]) and plan[part][j] == step:
                functions[part](j)


def build_layer(nc, x, rel_table, bucket_onehot, attn_norm_g, ffn_norm_g, w_qkv, w_o, q_gain, k_gain,
                lam_q1, lam_k1, lam_q2, lam_k2, sub_gain, w_in, conv_w, conv_b, w_out, out):
    S, D = x.shape[1], x.shape[2]
    NB = S // P
    KC = D // P
    MAPS = D // HEAD_DIM
    HEADS = MAPS // 2
    VD = 2 * HEAD_DIM
    FF = w_out.shape[1]
    FC = FF // P
    BUCKETS = rel_table.shape[0]
    TAPS = conv_w.shape[1]
    assert (S, D, VD, TAPS) == (2 * P, 2048, P, 3)

    QKV_GROUPS = HEADS // 2
    QW = 2 * VD
    FFN_BLOCKS = 4
    FFN_GROUPS = FC // FFN_BLOCKS
    HALF = D // 2
    O_BASE = QKV_GROUPS * KC
    IN_BASE = O_BASE + 2 * HEADS
    OUT_BASE = IN_BASE + FFN_GROUPS * KC
    assert not (O_BASE % RAW_SLOTS or IN_BASE % RAW_SLOTS or OUT_BASE % RAW_SLOTS or KC % RAW_SLOTS)
    PIECES = KC // 4
    GROUP_RSTD = NB * 8
    TABLE_W = S + P
    BIAS_COPIES = 32
    CONV_STEP = 10

    with ExitStack() as ctx:
        def sb(name, shape, dt=F32):
            return ctx.enter_context(nc.sbuf_tensor(name, shape, dt))

        def sem(name):
            return ctx.enter_context(nc.semaphore(name))

        resid = sb("resid", [P, NB, D])
        act_hi = sb("act_hi", [P, KC, S], F32R)
        act_lo = sb("act_lo", [P, KC, S], F32R)
        weight_raw = sb("weight_raw", [P, RAW_SLOTS, SUB])
        weight_hi = sb("weight_hi", [P, SPLIT_SLOTS, SUB], F32R)
        weight_lo = sb("weight_lo", [P, SPLIT_SLOTS, SUB], F32R)
        chunk_hi = sb("chunk_hi", [P, SPLIT_SLOTS, S], F32R)
        chunk_lo = sb("chunk_lo", [P, SPLIT_SLOTS, S], F32R)
        shared = sb("shared", [P, FC * S + D])
        pos_bias = shared[:, 0:MAPS * S].rearrange("p (m k) -> p m k", k=S)
        attn_out = shared[:, MAPS * S:MAPS * S + HEADS * S].rearrange("p (h t) -> p h t", t=S)
        hidden = shared[:, 0:FC * S].rearrange("p (c t) -> p c t", t=S)
        scaled = shared[:, FC * S:FC * S + D]
        work = sb("work", [P, 5120])
        qk = work[:, 0:1024].rearrange("p (b c) -> p b c", b=NB)
        qk_sq = work[:, 1024:2048]
        scores1 = work[:, 1024:2048].rearrange("p (j m k) -> p j m k", j=2, m=2)
        v_sb = work[:, 2048:2560].rearrange("p (b c) -> p b c", b=NB)
        qT = work[:, 2560:3072].rearrange("p (j t) -> p j t", j=2)
        kT = work[:, 3072:3584].rearrange("p (j t) -> p j t", j=2)
        scores0 = work[:, 3584:4096].rearrange("p (j m k) -> p j m k", j=2, m=2)
        probsT = work[:, 4096:4864].rearrange("p (j c q) -> p j c q", j=2, c=3)
        o_junk = work[:, 4864:5120]
        gain_all = work[:, 2048:2048 + D]
        norm_junk = work[:, 4096:5120]
        conv_rows = work[0:2 * FC, 0:(TAPS + 1) * P].rearrange("c (t p) -> c t p", p=P)
        onehot_sb = work[0:BUCKETS, 512:512 + S]
        bias_rows = work[0:MAPS, 768:768 + TABLE_W]
        pre_gate = work[:, 0:FFN_BLOCKS * S].rearrange("p (i t) -> p i t", t=S)
        pre_up = work[:, FFN_BLOCKS * S:2 * FFN_BLOCKS * S].rearrange("p (i t) -> p i t", t=S)
        head_out = sb("head_out", [P, 2, NB, VD])
        ident = sb("ident", [P, P])
        ones_row = sb("ones_row", [1, P])
        warm_up = sb("warm_up", [1, 1])
        table_sb = sb("table_sb", [BUCKETS, MAPS])
        conv_cols = sb("conv_cols", [P, TAPS + 1, 2 * FC])
        gains = sb("gains", [P, 5])
        lam_vecs = sb("lam_vecs", [P, 4, HEAD_DIM])
        lam_prod = sb("lam_prod", [P, 2, HEAD_DIM])
        lam_dot = sb("lam_dot", [P, 2])
        lam_exp = sb("lam_exp", [P, 2])
        lam_diff = sb("lam_diff", [P, 1])
        neg_lam = sb("neg_lam", [P, 1])
        norm_sq = sb("norm_sq", [P, NB, 4])
        norm_sum = sb("norm_sum", [P, NB])
        norm_ms = sb("norm_ms", [P, NB])
        norm_rstd = sb("norm_rstd", [P, NB])
        power = sb("power", [P, GROUP_RSTD])
        eps = sb("eps", [P, GROUP_RSTD])
        qk_ss = sb("qk_ss", [P, GROUP_RSTD])
        qk_ms = sb("qk_ms", [P, GROUP_RSTD])
        qk_rstd = sb("qk_rstd", [P, GROUP_RSTD])
        neg_max = sb("neg_max", [P, 2, 4])
        exp_sum = sb("exp_sum", [P, 2, 4])
        coef = sb("coef", [P, 2, 4])
        o_ss = sb("o_ss", [P, 2, NB])
        o_ms = sb("o_ms", [P, 2, NB])
        o_rstd = sb("o_rstd", [P, 2, NB])

        psum = ctx.enter_context(nc.psum_tensor("psum", [P, 8, BANK], F32))
        ps_qkT = psum[:, 4, :]
        ps_o = psum[:, 4, 0:S].rearrange("p (b e) -> p b e", b=NB)
        ps_s1 = psum[:, 5:7, 0:S]
        ps_s0 = psum[:, 5:7, S:S + P]
        ps_pT = psum[:, 7, 0:3 * P].rearrange("p (c q) -> p c q", c=3)
        ps_oT = psum[:, 7, 0:S]
        bias_scratch = nc.dram_tensor("bias_scratch", [MAPS, TABLE_W], F32, kind="Internal").ap()
        bias_copies = nc.dram_tensor("bias_copies", [BIAS_COPIES, MAPS, TABLE_W], F32, kind="Internal").ap()

        raw_landed = [sem(f"raw_landed{i}") for i in range(RAW_SLOTS)]
        hi_ready = sem("hi_ready")
        lo_ready = sem("lo_ready")
        weights_used = sem("weights_used")
        chunk_hi_ready = sem("chunk_hi_ready")
        chunk_lo_ready = sem("chunk_lo_ready")
        x_landed = [sem(f"x_landed{i}") for i in range(2 * NB)]
        gain_landed = [sem("attn_gain_landed"), sem("ffn_gain_landed")]
        small_landed = sem("small_landed")
        conv_landed = sem("conv_landed")
        table_landed = sem("table_landed")
        ones_ready = sem("ones_ready")
        warmed_up = sem("warmed_up")
        gain_spread = sem("gain_spread")
        gain_stored = sem("gain_stored")
        ident_zero = sem("ident_zero")
        ident_ready = sem("ident_ready")
        power_ready = sem("power_ready")
        mask_ready = sem("mask_ready")
        table_summed = sem("table_summed")
        table_stored = sem("table_stored")
        bias_written = sem("bias_written")
        bias_copied = sem("bias_copied")
        bias_landed = sem("bias_landed")
        conv_turned = sem("conv_turned")
        conv_stored = sem("conv_stored")
        gains_step = sem("gains_step")
        lam_step = sem("lam_step")
        lam_exped = sem("lam_exped")
        norm_squared = sem("norm_squared")
        norm_summed = sem("norm_summed")
        norm_ms_ready = sem("norm_ms_ready")
        norm_rstd_ready = sem("norm_rstd_ready")
        norm_scaled = sem("norm_scaled")
        norm_turned = sem("norm_turned")
        norm_hi_ready = sem("norm_hi_ready")
        norm_lo_ready = sem("norm_lo_ready")
        qk_summed = sem("qk_summed")
        qk_stored = sem("qk_stored")
        v_stored = sem("v_stored")
        qk_squared = sem("qk_squared")
        qk_ss_ready = sem("qk_ss_ready")
        qk_ms_ready = sem("qk_ms_ready")
        qk_rstd_ready = sem("qk_rstd_ready")
        qk_normed = sem("qk_normed")
        qk_turned = sem("qk_turned")
        qkT_stored = sem("qkT_stored")
        scores_done = sem("scores_done")
        scores_biased = sem("scores_biased")
        neg_max_ready = sem("neg_max_ready")
        exps_done = sem("exps_done")
        recip_ready = sem("recip_ready")
        coef_ready = sem("coef_ready")
        second_scaled = sem("second_scaled")
        probs_ready = sem("probs_ready")
        probs_turned = sem("probs_turned")
        probsT_stored = sem("probsT_stored")
        values_summed = sem("values_summed")
        o_squared = sem("o_squared")
        o_ms_ready = sem("o_ms_ready")
        o_rstd_ready = sem("o_rstd_ready")
        o_normed = sem("o_normed")
        o_turned = sem("o_turned")
        oT_stored = sem("oT_stored")
        proj_summed = sem("proj_summed")
        resid_added = sem("resid_added")
        ffn_summed = sem("ffn_summed")
        conv_tap2 = sem("conv_tap2")
        conv_tap1 = sem("conv_tap1")
        conv_done = sem("conv_done")
        gate_ready = sem("gate_ready")
        hidden_ready = sem("hidden_ready")
        out_landed = [sem(f"out_landed{half}") for half in range(2)]

        qkv_rows = w_qkv[0].rearrange("(k p) (s c) -> k p s c", p=P, s=3)
        o_rows = w_o[0].rearrange("(k p) (h c) -> k h p c", p=P, h=2)
        in_rows = w_in[0].rearrange("(k p) (s c) -> k p s c", p=P, s=2)
        out_rows = w_out[0].rearrange("(k p) (h c) -> k h p c", p=P, h=2)
        x_rows = x[0].rearrange("(b p) d -> b p d", p=P)
        result_rows = out[0].rearrange("(b p) d -> b p d", p=P)

        def on_all(vector, n):
            return bass.AP(tensor=vector.tensor, offset=vector.offset, ap=[[0, P], [1, n]])

        def projection_banks(first):
            return [(first + 2 * b + c, b, c) for b in range(NB) for c in range(2)]

        O_FIRST_BANK = (0, 4)
        OUT_FIRST_BANK = (4, 0)

        def piece(q):
            i, b = divmod(q, NB)
            slot = q % 4
            return slice(4 * i, 4 * i + 4), slice(b * P, (b + 1) * P), 4 + slot, slice(slot * BANK, (slot + 1) * BANK)

        def store_half(eng, half):
            for i, (_, b, c) in enumerate(projection_banks(0)):
                eng.wait_ge(resid_added, (2 + half) * 2 * NB + i + 1)
                cols = slice(half * HALF + c * BANK, half * HALF + (c + 1) * BANK)
                eng.dma_start(result_rows[b][:, cols], resid[:, b, cols]).then_inc(out_landed[half], 16)

        block = ctx.enter_context(nc.Block())

        @block.sync
        def _(sp):
            def load(n, slot, dst_cols, src, first=False):
                if not first:
                    sp.wait_ge(lo_ready, n - RAW_SLOTS + 1)
                dst = weight_raw[:, slot, 0:dst_cols]
                if len(src.shape) == 3:
                    dst = dst.rearrange("p (s c) -> p s c", s=src.shape[1])
                sp.dma_start(dst, src).then_inc(raw_landed[slot], 16)

            def load_qkv(g, k, first=False):
                load(g * KC + k, k % RAW_SLOTS, 3 * QW, qkv_rows[k][:, :, bass.ds(g * QW, QW)], first)

            for b in range(NB):
                for i in range(2):
                    cols = slice(i * HALF, (i + 1) * HALF)
                    sp.dma_start(resid[:, b, cols], x_rows[b][:, cols]).then_inc(x_landed[NB * b + i], 16)
            for k in range(RAW_SLOTS):
                load_qkv(0, k, first=True)
            for t in range(TAPS):
                sp.dma_start(conv_rows[:, t, :], conv_w[0, t].rearrange("(c p) -> c p", p=P)).then_inc(conv_landed, 16)
            sp.dma_start(conv_rows[:, TAPS, :], conv_b[0].rearrange("(c p) -> c p", p=P)).then_inc(conv_landed, 16)
            for m in range(2):
                rows = slice(m * HEAD_DIM, (m + 1) * HEAD_DIM)
                sp.dma_start(gains[rows, 0:1], q_gain[0].rearrange("(d a) -> d a", a=1)).then_inc(small_landed, 16)
                sp.dma_start(gains[rows, 1:2], k_gain[0].rearrange("(d a) -> d a", a=1)).then_inc(small_landed, 16)
            sp.dma_start(gains[:, 3:4], sub_gain[0].rearrange("(d a) -> d a", a=1)).then_inc(small_landed, 16)
            for i, vec in enumerate((lam_q1, lam_k1, lam_q2, lam_k2)):
                sp.dma_start(lam_vecs[:, i, :], on_all(vec, HEAD_DIM)).then_inc(small_landed, 16)
            for k in range(RAW_SLOTS, KC):
                load_qkv(0, k)
            with sp.Fori(1, QKV_GROUPS) as g:
                for k in range(KC):
                    load_qkv(g, k)
            for half in range(2):
                with sp.Fori(0, HEADS // RAW_SLOTS) as i:
                    for j in range(RAW_SLOTS):
                        load(O_BASE + half * HEADS + i * RAW_SLOTS + j, j, SUB,
                             o_rows[bass.ds(i * RAW_SLOTS + j, 1), half, :, :].squeeze(0))
                if half == 1:
                    sp.wait_ge(oT_stored, HEADS)
                    sp.dma_start(gain_all, on_all(ffn_norm_g, D)).then_inc(gain_landed[1], 16)
            with sp.Fori(0, FFN_GROUPS) as g:
                for k in range(KC):
                    load(IN_BASE + g * KC + k, k % RAW_SLOTS, SUB, in_rows[k][:, :, bass.ds(g * BANK, BANK)])
            with sp.Fori(0, FC // RAW_SLOTS) as i:
                for j in range(RAW_SLOTS):
                    load(OUT_BASE + i * RAW_SLOTS + j, j, SUB,
                         out_rows[bass.ds(i * RAW_SLOTS + j, 1), 0, :, :].squeeze(0))
            rest = FC % RAW_SLOTS
            for j in range(rest):
                load(OUT_BASE + FC - rest + j, j, SUB, out_rows[FC - rest + j, 0])
            for j in range(rest):
                load(OUT_BASE + FC + j, rest + j, SUB, out_rows[j, 1])
            with sp.Fori(0, FC // RAW_SLOTS) as i:
                for j in range(RAW_SLOTS):
                    load(OUT_BASE + FC + rest + i * RAW_SLOTS + j, j, SUB,
                         out_rows[bass.ds(i * RAW_SLOTS + j + rest, 1), 1, :, :].squeeze(0))
            store_half(sp, 1)
            for half in range(2):
                sp.wait_ge(out_landed[half], 2 * NB * 16)

        @block.gpsimd
        def _(pool):
            pool.memset(ones_row[:, :], 1.0).then_inc(ones_ready, 1)
            pool.memset(ident[:, :], 0.0).then_inc(ident_zero, 1)
            pool.memset(power[:, :], -0.5).then_inc(power_ready, 1)
            pool.memset(eps[:, :], EPS).then_inc(power_ready, 1)
            pool.memset(bias_rows[:, S:TABLE_W], MASKED).then_inc(mask_ready, 1)
            pool.wait_ge(ident_zero, 1)
            pool.affine_select(out=ident[:, :], in_=ident[:, :], compare_op=ALU.not_equal, fill=1.0, base=0,
                               pattern=[[-1, P]], channel_multiplier=1).then_inc(ident_ready, 1)
            pool.wait_ge(power_ready, 2)

            def norm_rstd_step(which, b):
                n = which * NB + b + 1
                pool.wait_ge(norm_summed, n)
                pool.tensor_tensor(norm_ms[:, b:b + 1], norm_sum[:, b:b + 1], eps[:, b:b + 1],
                                   ALU.add).then_inc(norm_ms_ready, 1)
                pool.wait_ge(norm_ms_ready, n)
                pool.tensor_tensor(norm_rstd[:, b:b + 1], norm_ms[:, b:b + 1], power[:, b:b + 1],
                                   ALU.pow).then_inc(norm_rstd_ready, 1)

            def attention_rstds(g):
                pool.wait_ge(qk_ss_ready, g + 1)
                pool.tensor_tensor(qk_ms[:, :], qk_ss[:, :], eps[:, :], ALU.add).then_inc(qk_ms_ready, 1)
                pool.wait_ge(qk_ms_ready, g + 1)
                pool.tensor_tensor(qk_rstd[:, :], qk_ms[:, :], power[:, :], ALU.pow).then_inc(qk_rstd_ready, 1)
                for j in range(2):
                    pool.wait_ge(o_squared, 2 * g + j + 1)
                    pool.tensor_tensor(o_ms[:, j, :], o_ss[:, j, :], eps[:, 0:NB],
                                       ALU.add).then_inc(o_ms_ready, 1)
                    pool.wait_ge(o_ms_ready, 2 * g + j + 1)
                    pool.tensor_tensor(o_rstd[:, j, :], o_ms[:, j, :], power[:, 0:NB],
                                       ALU.pow).then_inc(o_rstd_ready, 1)

            for b in range(NB):
                norm_rstd_step(0, b)
            pool.wait_ge(table_stored, 1)
            pool.wait_ge(mask_ready, 1)
            pool.dma_start(bias_scratch, bias_rows).then_inc(bias_written, 16)
            pool.wait_ge(bias_written, 16)
            pool.dma_start(bias_copies, bass.AP(tensor=bias_scratch.tensor, offset=0,
                                                ap=[[0, BIAS_COPIES], [TABLE_W, MAPS],
                                                    [1, TABLE_W]])).then_inc(bias_copied, 16)
            pool.wait_ge(bias_copied, 16)
            for first in range(0, P, BIAS_COPIES):
                pool.dma_start(pos_bias[first:first + BIAS_COPIES, :, :],
                               bass.AP(tensor=bias_copies.tensor, offset=P - 1 - first,
                                       ap=[[MAPS * TABLE_W - 1, BIAS_COPIES], [TABLE_W, MAPS],
                                           [1, S]])).then_inc(bias_landed, 16)
            with pool.Fori(0, QKV_GROUPS) as g:
                attention_rstds(g)
            for b in range(NB):
                norm_rstd_step(1, b)
            store_half(pool, 0)

        @block.scalar
        def _(act):
            act.dma_start(gain_all[0:1, :], attn_norm_g).then_inc(gain_landed[0], 16)
            act.dma_start(table_sb[:, :], rel_table).then_inc(table_landed, 16)
            act.dma_start(onehot_sb, bucket_onehot).then_inc(table_landed, 16)
            act.wait_ge(ones_ready, 1)
            act.activation(warm_up[:, :], ones_row[:, 0:1], ACT.Square).then_inc(warmed_up, 1)

            def split_weights(n, slot, cols):
                act.wait_ge(raw_landed[slot % RAW_SLOTS], (n - slot % RAW_SLOTS) * (16 // RAW_SLOTS) + 16)
                if not (isinstance(n, int) and n < SPLIT_SLOTS):
                    act.wait_ge(weights_used, n - SPLIT_SLOTS + 1)
                act.activation(weight_hi[:, slot % SPLIT_SLOTS, 0:cols], weight_raw[:, slot % RAW_SLOTS, 0:cols],
                               ACT.Copy).then_inc(hi_ready, 1)

            def split_chunk(slot, src):
                act.activation(chunk_hi[:, slot % SPLIT_SLOTS, :], src, ACT.Copy).then_inc(chunk_hi_ready, 1)

            def norm_squares(n, b, piece, cols):
                if n:
                    act.wait_ge(norm_squared, n)
                act.activation(norm_junk[:, 0:cols.stop - cols.start], resid[:, b, cols], ACT.Square, scale=D ** -0.5,
                               accum_out=norm_sq[:, b, piece:piece + 1]).then_inc(norm_squared, 1)

            def norm_hi(which, q):
                chunks, tokens, bank, _ = piece(q)
                act.wait_ge(norm_turned, which * NB * PIECES + q + 1)
                act.activation(act_hi[:, chunks, tokens], psum[:, bank, :].rearrange("p (c t) -> p c t", t=P),
                               ACT.Copy).then_inc(norm_hi_ready, 1)

            def attention(g, step, plan):
                def store_qk(_):
                    for b in range(NB):
                        act.wait_ge(qk_summed, NB * g + b + 1)
                        act.activation(qk[:, b, :], psum[:, b, :], ACT.Copy).then_inc(qk_stored, 1)
                    act.wait_ge(qk_stored, NB * g + NB)
                    act.activation(qk_sq, qk.rearrange("p b c -> p (b c)"), ACT.Square,
                                   scale=HEAD_DIM ** -0.5).then_inc(qk_squared, 1)

                def store_qkT(j):
                    act.wait_ge(qk_turned, 2 * g + j + 1)
                    act.activation(qT[:, j, :], ps_qkT[:, 0:S], ACT.Copy, scale=gains[:, 2:3])
                    act.activation(kT[:, j, :], ps_qkT[:, S:2 * S], ACT.Copy).then_inc(qkT_stored, 1)

                def exps(j):
                    act.wait_ge(neg_max_ready, 2 * g + j + 1)
                    for m in range(2):
                        act.activation(scores1[:, j, m, :], scores1[:, j, m, :], ACT.Exp,
                                       bias=neg_max[:, j, 2 + m:3 + m], accum_out=exp_sum[:, j, 2 + m:3 + m])
                    for m in range(2):
                        ins = act.activation(scores0[:, j, m, :], scores0[:, j, m, :], ACT.Exp,
                                             bias=neg_max[:, j, m:m + 1], accum_out=exp_sum[:, j, m:m + 1])
                    ins.then_inc(exps_done, 1)

                def store_probsT(j):
                    act.wait_ge(probs_turned, 2 * g + j + 1)
                    act.activation(probsT[:, j, :, :], ps_pT, ACT.Copy).then_inc(probsT_stored, 1)

                def square_o(j):
                    act.wait_ge(values_summed, 2 * g + j + 1)
                    for b in range(NB):
                        ins = act.activation(o_junk[:, b * VD:(b + 1) * VD], ps_o[:, b, :], ACT.Square, scale=VD ** -0.5,
                                             accum_out=o_ss[:, j, b:b + 1])
                    ins.then_inc(o_squared, 1)

                def store_oT(j):
                    act.wait_ge(o_turned, 2 * g + j + 1)
                    act.activation(attn_out[:, bass.ds(2 * g + j, 1), :].squeeze(1), ps_oT, ACT.Copy,
                                   scale=gains[:, 4:5]).then_inc(oT_stored, 1)

                run_plan(plan, ACT_PARTS, step, dict(store_qk=store_qk, store_qkT=store_qkT, exps=exps,
                                                     store_probsT=store_probsT, square_o=square_o,
                                                     store_oT=store_oT))

            def convolve(g, bank, first_bank):
                if bank < 3:
                    act.wait_ge(ffn_summed, 3 * g + bank + 1)
                else:
                    act.wait_ge(weights_used, IN_BASE + (g + 1) * KC)
                for u in range(2):
                    i = 2 * bank + u
                    col = (FC if i >= FFN_BLOCKS else 0) + g * FFN_BLOCKS + i % FFN_BLOCKS
                    dst = (pre_gate if i < FFN_BLOCKS else pre_up)[:, i % FFN_BLOCKS, :]
                    ins = act.activation(dst, psum[:, first_bank + bank, u * S:(u + 1) * S], ACT.Identity,
                                         bias=conv_cols[:, TAPS, bass.ds(col, 1)],
                                         scale=conv_cols[:, TAPS - 1, bass.ds(col, 1)])
                ins.then_inc(conv_tap2, 1)

            def hidden_step(g, step, first_bank):
                if 2 <= step < 6:
                    convolve(g, step - 2, first_bank)
                if step == 6:
                    act.wait_ge(conv_done, 4 * g + 2)
                    act.activation(pre_gate, pre_gate, ACT.Silu).then_inc(gate_ready, 1)

            for b in range(NB):
                for i in range(2):
                    act.wait_ge(x_landed[NB * b + i], 16)
                    norm_squares(NB * b + i, b, i, slice(i * HALF, (i + 1) * HALF))
            norm_hi(0, 0)
            split_weights(0, 0, 3 * QW)
            split_weights(1, 1, 3 * QW)
            norm_hi(0, 1)
            split_weights(2, 2, 3 * QW)
            norm_hi(0, 2)
            norm_hi(0, 3)
            split_weights(3, 3, 3 * QW)
            for k in (4, 5):
                split_weights(k, k, 3 * QW)
                norm_hi(0, 2 * k - 4)
                norm_hi(0, 2 * k - 3)
            for k in range(6, KC):
                split_weights(k, k, 3 * QW)
                if k == CONV_STEP + 3:
                    act.wait_ge(conv_turned, 1)
                    act.activation(conv_cols[:, :, :],
                                   psum[:, 3, 0:(TAPS + 1) * 2 * FC].rearrange("p (t c) -> p t c", c=2 * FC),
                                   ACT.Copy).then_inc(conv_stored, 1)
            act.wait_ge(lam_step, 2)
            act.activation(lam_exp[:, :], lam_dot[:, :], ACT.Exp).then_inc(lam_exped, 1)
            act.wait_ge(bias_written, 16)
            with act.Fori(1, QKV_GROUPS) as g:
                for k in range(KC):
                    split_weights(g * KC + k, k, 3 * QW)
                    attention(g - 1, k, QKV_PLAN)
            for h in range(HEADS):
                split_weights(O_BASE + h, h, SUB)
                if h >= HEADS - 2:
                    act.wait_ge(oT_stored, h + 1)
                split_chunk(h, attn_out[:, h, :])
                attention(QKV_GROUPS - 1, h, O_PLAN)
            for h in range(HEADS):
                split_weights(O_BASE + HEADS + h, h, SUB)
                split_chunk(h, attn_out[:, h, :])
                if 4 <= h < 4 + 2 * NB:
                    i = h - 4
                    act.wait_ge(resid_added, i + 1)
                    norm_squares(4 + i, i // 2, i % 2, slice((i % 2) * BANK, (i % 2 + 1) * BANK))
            for n in range(3):
                split_weights(IN_BASE + n, n, SUB)
            for i in range(2 * NB):
                act.wait_ge(resid_added, 2 * NB + i + 1)
                norm_squares(8 + i, i // 2, 2 + i % 2, slice(HALF + (i % 2) * BANK, HALF + (i % 2 + 1) * BANK))
            for q in range(0, NB * PIECES, 2):
                norm_hi(1, q)
                norm_hi(1, q + 1)
                split_weights(IN_BASE + 3 + q // 2, 3 + q // 2, SUB)
            for k in range(3 + PIECES, KC):
                split_weights(IN_BASE + k, k, SUB)
            with act.Fori(0, FFN_GROUPS // 2) as pair:
                for odd in range(2):
                    for k in range(KC):
                        split_weights(IN_BASE + (pair * 2 + odd + 1) * KC + k, k, SUB)
                        hidden_step(pair * 2 + odd, k, 4 * odd)
            for j in range(RAW_SLOTS):
                split_weights(OUT_BASE + j, j, SUB)
                split_chunk(j, hidden[:, j, :])
                hidden_step(FFN_GROUPS - 1, j, 0)
            with act.Fori(1, FC // RAW_SLOTS) as i:
                for j in range(RAW_SLOTS):
                    split_weights(OUT_BASE + i * RAW_SLOTS + j, j, SUB)
                    split_chunk(j, hidden[:, bass.ds(i * RAW_SLOTS + j, 1), :].squeeze(1))
            rest = FC % RAW_SLOTS
            for j in range(rest):
                split_weights(OUT_BASE + FC - rest + j, j, SUB)
                if j == 0:
                    act.wait_ge(hidden_ready, FFN_GROUPS)
                split_chunk(j, hidden[:, FC - rest + j, :])
            for j in range(rest):
                split_weights(OUT_BASE + FC + j, rest + j, SUB)
                split_chunk(rest + j, hidden[:, j, :])
            with act.Fori(0, FC // RAW_SLOTS) as i:
                for j in range(RAW_SLOTS):
                    split_weights(OUT_BASE + FC + rest + i * RAW_SLOTS + j, j, SUB)
                    split_chunk(j, hidden[:, bass.ds(i * RAW_SLOTS + j + rest, 1), :].squeeze(1))

        @block.vector
        def _(dve):
            def split_weights(n, slot, cols):
                dve.wait_ge(hi_ready, n + 1)
                dve.tensor_tensor(weight_lo[:, slot % SPLIT_SLOTS, 0:cols], weight_raw[:, slot % RAW_SLOTS, 0:cols],
                                  weight_hi[:, slot % SPLIT_SLOTS, 0:cols].bitcast(F32),
                                  ALU.subtract).then_inc(lo_ready, 1)

            def split_chunk(m, slot, src):
                dve.wait_ge(chunk_hi_ready, m + 1)
                dve.tensor_tensor(chunk_lo[:, slot % SPLIT_SLOTS, :], src,
                                  chunk_hi[:, slot % SPLIT_SLOTS, :].bitcast(F32),
                                  ALU.subtract).then_inc(chunk_lo_ready, 1)

            def norm_total(which, b, pieces):
                dve.wait_ge(norm_squared, 2 * NB + 2 * NB + 2 * (b + 1) if which else 2 * (b + 1))
                dve.tensor_reduce(norm_sum[:, b:b + 1], norm_sq[:, b, 0:pieces], AX_X, ALU.add).then_inc(norm_summed, 1)

            def norm_scale(which, q):
                (i, b), n = divmod(q, NB), which * NB * PIECES + q
                dve.wait_ge(norm_rstd_ready, which * NB + b + 1)
                if q >= 4:
                    dve.wait_ge(norm_turned, n - 3)
                cols = slice(i * BANK, (i + 1) * BANK)
                dve.scalar_tensor_tensor(out=scaled[:, piece(q)[3]], in0=resid[:, b, cols],
                                         scalar=norm_rstd[:, b:b + 1], in1=gain_all[:, cols],
                                         op0=ALU.mult, op1=ALU.mult).then_inc(norm_scaled, 1)

            def norm_lo(which, q):
                chunks, tokens, bank, _ = piece(q)
                dve.wait_ge(norm_hi_ready, which * NB * PIECES + q + 1)
                dve.tensor_tensor(act_lo[:, chunks, tokens], psum[:, bank, :].rearrange("p (c t) -> p c t", t=P),
                                  act_hi[:, chunks, tokens].bitcast(F32), ALU.subtract).then_inc(norm_lo_ready, 1)

            def normalise(which, base, ahead, cols):
                n = ahead
                for q in range(4):
                    norm_scale(which, q)
                for q in range(0, NB * PIECES, 2):
                    if q >= 4:
                        norm_scale(which, q)
                        norm_scale(which, q + 1)
                        split_weights(base + n, n, cols)
                        n += 1
                    norm_lo(which, q)
                    norm_lo(which, q + 1)
                    if q == 0:
                        for _ in range(1 if ahead else 2):
                            split_weights(base + n, n, cols)
                            n += 1
                return n

            def attention(g, step, plan):
                def store_v(_):
                    dve.wait_ge(weights_used, (g + 1) * KC)
                    dve.tensor_copy(v_sb, psum[:, NB, :].rearrange("p (b c) -> p b c", b=NB)).then_inc(v_stored, 1)

                def sum_qk(_):
                    dve.wait_ge(qk_squared, g + 1)
                    dve.tensor_reduce(qk_ss[:, :], qk_sq.rearrange("p (m d) -> p m d", d=HEAD_DIM), AX_X,
                                      ALU.add).then_inc(qk_ss_ready, 1)

                def norm_qk(_):
                    dve.wait_ge(qk_rstd_ready, g + 1)
                    rows = qk.rearrange("p b (m d) -> p (b m) d", d=HEAD_DIM)
                    dve.tensor_tensor(rows, rows, qk_rstd[:, :].unsqueeze(2).to_broadcast([P, GROUP_RSTD, HEAD_DIM]),
                                      ALU.mult).then_inc(qk_normed, 1)

                def bias(j):
                    n = 2 * g + j + 1
                    dve.wait_ge(bias_landed, P // BIAS_COPIES * 16)
                    dve.wait_ge(scores_done, n)
                    maps = bass.ds(4 * g + 2 * j, 2)
                    dve.tensor_tensor(scores1[:, j, :, :], ps_s1, pos_bias[:, maps, :], ALU.add)
                    dve.tensor_tensor(scores0[:, j, :, :], ps_s0, pos_bias[:, maps, P:S],
                                      ALU.add).then_inc(scores_biased, 1)
                    dve.wait_ge(scores_biased, n)
                    dve.tensor_reduce(neg_max[:, j, 2:4], scores1[:, j, :, :], AX_X, ALU.max, negate=True)
                    dve.tensor_reduce(neg_max[:, j, 0:2], scores0[:, j, :, :], AX_X, ALU.max,
                                      negate=True).then_inc(neg_max_ready, 1)

                def combine(j):
                    n = 2 * g + j + 1
                    dve.wait_ge(exps_done, n)
                    dve.reciprocal(coef[:, j, :], exp_sum[:, j, :]).then_inc(recip_ready, 1)
                    dve.wait_ge(recip_ready, n)
                    second = coef[:, j, :].rearrange("p (b m) -> p b m", m=2)[:, :, 1]
                    dve.tensor_scalar(second, second, neg_lam[:, :], None, ALU.mult).then_inc(coef_ready, 1)
                    dve.wait_ge(coef_ready, n)
                    dve.tensor_scalar(scores1[:, j, 1, :], scores1[:, j, 1, :], coef[:, j, 3:4], None, ALU.mult)
                    dve.tensor_scalar(scores0[:, j, 1, :], scores0[:, j, 1, :], coef[:, j, 1:2], None,
                                      ALU.mult).then_inc(second_scaled, 1)
                    dve.wait_ge(second_scaled, n)
                    dve.scalar_tensor_tensor(out=scores1[:, j, 0, :], in0=scores1[:, j, 0, :],
                                             scalar=coef[:, j, 2:3], in1=scores1[:, j, 1, :],
                                             op0=ALU.mult, op1=ALU.add)
                    dve.scalar_tensor_tensor(out=scores0[:, j, 0, :], in0=scores0[:, j, 0, :],
                                             scalar=coef[:, j, 0:1], in1=scores0[:, j, 1, :],
                                             op0=ALU.mult, op1=ALU.add).then_inc(probs_ready, 1)

                def norm_o(j):
                    dve.wait_ge(o_rstd_ready, 2 * g + j + 1)
                    dve.tensor_tensor(head_out[:, j, :, :], ps_o,
                                      o_rstd[:, j, :].unsqueeze(2).to_broadcast([P, NB, VD]),
                                      ALU.mult).then_inc(o_normed, 1)

                run_plan(plan, DVE_PARTS, step, dict(store_v=store_v, sum_qk=sum_qk, norm_qk=norm_qk, bias=bias,
                                                     combine=combine, norm_o=norm_o))

            def convolve(g, bank, first_bank):
                n = 4 * g + bank + 1
                dve.wait_ge(conv_tap2, n)
                for tap in range(TAPS - 2, -1, -1):
                    shift = TAPS - 1 - tap
                    for u in range(2):
                        i = 2 * bank + u
                        col = (FC if i >= FFN_BLOCKS else 0) + g * FFN_BLOCKS + i % FFN_BLOCKS
                        dst = (pre_gate if i < FFN_BLOCKS else pre_up)[:, i % FFN_BLOCKS, shift:S]
                        ins = dve.scalar_tensor_tensor(
                            out=dst, in0=psum[:, first_bank + bank, u * S:(u + 1) * S - shift],
                            scalar=conv_cols[:, tap, bass.ds(col, 1)], in1=dst, op0=ALU.mult, op1=ALU.add)
                    ins.then_inc(conv_done if tap == 0 else conv_tap1, 1)
                    if tap:
                        dve.wait_ge(conv_tap1, n)

            def hidden_step(g, step, first_bank, steps):
                if step in steps[0:4]:
                    convolve(g, steps.index(step), first_bank)
                if step == steps[4]:
                    dve.wait_ge(gate_ready, g + 1)
                    dve.wait_ge(conv_done, 4 * g + 4)
                    dve.tensor_tensor(hidden[:, bass.ds(g * FFN_BLOCKS, FFN_BLOCKS), :], pre_gate, pre_up,
                                      ALU.mult).then_inc(hidden_ready, 1)

            def add_residual(half, i, first_bank, stage, used):
                bank, b, c = projection_banks(first_bank)[i]
                cols = slice(half * HALF + c * BANK, half * HALF + (c + 1) * BANK)
                if i < 2 * NB - 1:
                    dve.wait_ge(proj_summed, (2 * stage + half) * (2 * NB - 1) + i + 1)
                else:
                    dve.wait_ge(weights_used, used)
                dve.tensor_tensor(resid[:, b, cols], psum[:, bank, :], resid[:, b, cols],
                                  ALU.add).then_inc(resid_added, 1)

            def store_gain(q):
                dve.wait_ge(gain_spread, q + 1)
                dve.tensor_copy(gain_all[:, q * BANK:(q + 1) * BANK], psum[:, 4 + q, :]).then_inc(gain_stored, 1)

            def scale_first(q):
                dve.wait_ge(gain_stored, q // NB + 1)
                norm_scale(0, q)

            store_gain(0)
            store_gain(1)
            norm_total(0, 0, 2)
            scale_first(0)
            norm_total(0, 1, 2)
            norm_lo(0, 0)
            split_weights(0, 0, 3 * QW)
            scale_first(1)
            split_weights(1, 1, 3 * QW)
            store_gain(2)
            norm_lo(0, 1)
            scale_first(2)
            store_gain(3)
            split_weights(2, 2, 3 * QW)
            scale_first(3)
            norm_lo(0, 2)
            split_weights(3, 3, 3 * QW)
            norm_lo(0, 3)
            dve.wait_ge(table_summed, 1)
            dve.tensor_copy(bias_rows[:, 0:S], psum[0:MAPS, 3, 0:S]).then_inc(table_stored, 1)
            for k in (4, 5):
                for q in (2 * k - 4, 2 * k - 3):
                    scale_first(q)
                split_weights(k, k, 3 * QW)
                for q in (2 * k - 4, 2 * k - 3):
                    norm_lo(0, q)
            for k in range(6, KC):
                split_weights(k, k, 3 * QW)
            dve.wait_ge(small_landed, 9 * 16)
            dve.tensor_tensor(gains[:, 2:3], gains[:, 0:1], gains[:, 1:2], ALU.mult).then_inc(gains_step, 1)
            dve.tensor_scalar(gains[:, 4:5], gains[:, 3:4], 1.0 - LAM_INIT, None, ALU.mult).then_inc(gains_step, 1)
            lam_pairs = lam_vecs[:, :, :].rearrange("p (i s) d -> p i s d", s=2)
            dve.tensor_tensor(lam_prod[:, :, :], lam_pairs[:, :, 0, :], lam_pairs[:, :, 1, :],
                              ALU.mult).then_inc(lam_step, 1)
            dve.wait_ge(gains_step, 2)
            dve.tensor_scalar(gains[:, 2:3], gains[:, 2:3], HEAD_DIM ** -0.5, None, ALU.mult).then_inc(gains_step, 1)
            dve.wait_ge(lam_step, 1)
            dve.tensor_reduce(lam_dot[:, :], lam_prod[:, :, :], AX_X, ALU.add).then_inc(lam_step, 1)
            dve.wait_ge(lam_exped, 1)
            dve.tensor_tensor(lam_diff[:, :], lam_exp[:, 1:2], lam_exp[:, 0:1], ALU.subtract).then_inc(lam_step, 1)
            dve.wait_ge(lam_step, 3)
            dve.tensor_scalar(neg_lam[:, :], lam_diff[:, :], LAM_INIT, None, ALU.subtract).then_inc(lam_step, 1)
            dve.wait_ge(lam_step, 4)
            with dve.Fori(1, QKV_GROUPS) as g:
                for k in range(KC):
                    split_weights(g * KC + k, k, 3 * QW)
                    attention(g - 1, k, QKV_PLAN)
            for h in range(HEADS):
                split_weights(O_BASE + h, h, SUB)
                split_chunk(h, h, attn_out[:, h, :])
                attention(QKV_GROUPS - 1, h, O_PLAN)
            for h in range(HEADS):
                split_weights(O_BASE + HEADS + h, h, SUB)
                split_chunk(HEADS + h, h, attn_out[:, h, :])
                if 3 <= h < 3 + 2 * NB:
                    add_residual(0, h - 3, O_FIRST_BANK[0], 0, O_BASE + HEADS)
            for n in range(3):
                split_weights(IN_BASE + n, n, SUB)
            for i in range(2 * NB):
                add_residual(1, i, O_FIRST_BANK[1], 0, IN_BASE)
            for b in range(NB):
                norm_total(1, b, 4)
            dve.wait_ge(gain_landed[1], 16)
            done = normalise(1, IN_BASE, 3, SUB)
            for k in range(done, KC):
                split_weights(IN_BASE + k, k, SUB)
            with dve.Fori(0, FFN_GROUPS // 2) as pair:
                for odd in range(2):
                    for k in range(KC):
                        split_weights(IN_BASE + (pair * 2 + odd + 1) * KC + k, k, SUB)
                        hidden_step(pair * 2 + odd, k, 4 * odd, (3, 5, 7, 9, 10))
            for j in range(RAW_SLOTS):
                split_weights(OUT_BASE + j, j, SUB)
                split_chunk(2 * HEADS + j, j, hidden[:, j, :])
                hidden_step(FFN_GROUPS - 1, j, 0, (3, 4, 5, 6, 7))
            with dve.Fori(1, FC // RAW_SLOTS) as i:
                for j in range(RAW_SLOTS):
                    split_weights(OUT_BASE + i * RAW_SLOTS + j, j, SUB)
                    split_chunk(2 * HEADS + i * RAW_SLOTS + j, j, hidden[:, bass.ds(i * RAW_SLOTS + j, 1), :].squeeze(1))
            rest = FC % RAW_SLOTS
            for j in range(rest):
                split_weights(OUT_BASE + FC - rest + j, j, SUB)
                split_chunk(2 * HEADS + FC - rest + j, j, hidden[:, FC - rest + j, :])
            for j in range(rest):
                split_weights(OUT_BASE + FC + j, rest + j, SUB)
                split_chunk(2 * HEADS + FC + j, rest + j, hidden[:, j, :])
                if j >= rest - 2:
                    for i in range(NB):
                        add_residual(0, NB * (j - rest + 2) + i, OUT_FIRST_BANK[0], 1, OUT_BASE + FC)
            with dve.Fori(0, FC // RAW_SLOTS) as i:
                for j in range(RAW_SLOTS):
                    split_weights(OUT_BASE + FC + rest + i * RAW_SLOTS + j, j, SUB)
                    split_chunk(2 * HEADS + FC + rest + i * RAW_SLOTS + j, j,
                                hidden[:, bass.ds(i * RAW_SLOTS + j + rest, 1), :].squeeze(1))
            for i in range(2 * NB):
                add_residual(1, i, OUT_FIRST_BANK[1], 1, OUT_BASE + 2 * FC)

        @block.tensor
        def _(pe):
            def product(dst, left, right, start, stop):
                (left_hi, left_lo), (right_hi, right_lo) = left, right
                pe.matmul(dst, left_hi, right_hi, start=start, stop=False, skip_group_check=True)
                pe.matmul(dst, left_hi, right_lo, start=False, stop=False, skip_group_check=True)
                return pe.matmul(dst, left_lo, right_hi, start=False, stop=stop, skip_group_check=True)

            def act_part(k, tokens):
                return act_hi[:, k, tokens], act_lo[:, k, tokens]

            def weight_part(slot, cols):
                return weight_hi[:, slot % SPLIT_SLOTS, cols], weight_lo[:, slot % SPLIT_SLOTS, cols]

            def queries_keys(k, b):
                return product(psum[:, b, :], act_part(k, slice(b * P, (b + 1) * P)),
                               weight_part(k, slice(0, 2 * QW)), k == 0, k == KC - 1)

            def value_rows(k, b):
                return product(psum[:, NB, b * QW:(b + 1) * QW], act_part(k, slice(b * P, (b + 1) * P)),
                               weight_part(k, slice(2 * QW, 3 * QW)), k == 0 and b == 0, k == KC - 1)

            def qkv(g, k, first=False):
                pe.wait_ge(lo_ready, g * KC + k + 1)
                for b in range(NB):
                    if k == 0 and not first:
                        pe.wait_ge(qk_stored, NB * (g - 1) + b + 1)
                    mm = queries_keys(k, b)
                    if k == KC - 1:
                        mm.then_inc(qk_summed, 1)
                if k == 0 and not first:
                    pe.wait_ge(v_stored, g)
                for b in range(NB):
                    mm = value_rows(k, b)
                mm.then_inc(weights_used, 1)

            def norm_turn(which, q):
                _, _, bank, cols = piece(q)
                n = which * NB * PIECES + q
                pe.wait_ge(norm_scaled, n + 1)
                if q >= 4:
                    pe.wait_ge(norm_lo_ready, n - 3)
                for c in range(4):
                    mm = turn(psum[:, bank, c * P:(c + 1) * P], scaled[:, cols][:, c * P:(c + 1) * P])
                mm.then_inc(norm_turned, 1)

            def norm_step(which, k):
                if k == 0:
                    for q in range(4):
                        norm_turn(which, q)
                if k in (2, 3):
                    for q in (2 * k, 2 * k + 1):
                        norm_turn(which, q)
                if k % 4 == 0:
                    pe.wait_ge(norm_lo_ready, (which * PIECES + k // 4 + 1) * NB)

            def turn(dst, src, k=P):
                return pe.transpose(dst, src, ident[0:k, 0:k])

            def attention(g, step, plan):
                def turn_qk(j):
                    pe.wait_ge(qk_normed, g + 1)
                    if j == 1:
                        pe.wait_ge(qkT_stored, 2 * g + 1)
                    for part in range(2):
                        for b in range(NB):
                            cols = slice(part * QW + j * VD, part * QW + (j + 1) * VD)
                            mm = turn(ps_qkT[:, part * S + b * P:part * S + (b + 1) * P], qk[:, b, cols])
                    mm.then_inc(qk_turned, 1)

                def score(j):
                    pe.wait_ge(qkT_stored, 2 * g + j + 1)
                    if j == 1:
                        pe.wait_ge(scores_biased, 2 * g + 1)
                    for m in range(2):
                        rows = slice(m * HEAD_DIM, (m + 1) * HEAD_DIM)
                        pe.matmul(ps_s1[:, m, :], qT[rows, j, P:S], kT[rows, j, :], start=True, stop=True)
                    for m in range(2):
                        rows = slice(m * HEAD_DIM, (m + 1) * HEAD_DIM)
                        mm = pe.matmul(ps_s0[:, m, :], qT[rows, j, 0:P], kT[rows, j, 0:P], start=True, stop=True)
                    mm.then_inc(scores_done, 1)

                def turn_probs(j):
                    pe.wait_ge(probs_ready, 2 * g + j + 1)
                    if j == 1:
                        pe.wait_ge(probsT_stored, 2 * g + 1)
                    for c in range(NB):
                        turn(ps_pT[:, c, :], scores1[:, j, 0, c * P:(c + 1) * P])
                    turn(ps_pT[:, NB, :], scores0[:, j, 0, :]).then_inc(probs_turned, 1)

                def values(j):
                    pe.wait_ge(probsT_stored, 2 * g + j + 1)
                    if j == 0:
                        pe.wait_ge(qkT_stored, 2 * g + 2)
                    else:
                        pe.wait_ge(o_normed, 2 * g + 1)
                    cols = slice(j * VD, (j + 1) * VD)
                    pe.matmul(ps_o[:, 0, :], probsT[:, j, NB, :], v_sb[:, 0, cols], start=True, stop=True)
                    pe.matmul(ps_o[:, 1, :], probsT[:, j, 0, :], v_sb[:, 0, cols], start=True, stop=False)
                    pe.matmul(ps_o[:, 1, :], probsT[:, j, 1, :], v_sb[:, 1, cols], start=False,
                              stop=True).then_inc(values_summed, 1)

                def turn_o(j):
                    pe.wait_ge(o_normed, 2 * g + j + 1)
                    if j == 0:
                        pe.wait_ge(probsT_stored, 2 * g + 2)
                    else:
                        pe.wait_ge(oT_stored, 2 * g + 1)
                    turn(ps_oT[:, 0:P], head_out[:, j, 0, :])
                    turn(ps_oT[:, P:S], head_out[:, j, 1, :]).then_inc(o_turned, 1)

                run_plan(plan, PE_PARTS, step, dict(turn_qk=turn_qk, score=score, turn_probs=turn_probs,
                                                    values=values, turn_o=turn_o))

            def project(n, m, slot, banks, start=False, stop=False, free=None):
                pe.wait_ge(lo_ready, n + 1)
                pe.wait_ge(chunk_lo_ready, m + 1)
                for i, (bank, b, c) in enumerate(banks):
                    if start and free:
                        free(i)
                    tokens = slice(b * P, (b + 1) * P)
                    s = slot % SPLIT_SLOTS
                    mm = product(psum[:, bank, :], (chunk_hi[:, s, tokens], chunk_lo[:, s, tokens]),
                                 weight_part(slot, slice(c * BANK, (c + 1) * BANK)), start, stop)
                    if stop and i < 2 * NB - 1:
                        mm.then_inc(proj_summed, 1)
                mm.then_inc(weights_used, 1)

            def ffn_in(g, k, first_bank):
                pe.wait_ge(lo_ready, IN_BASE + g * KC + k + 1)
                for i in range(2 * FFN_BLOCKS):
                    mm = product(psum[:, first_bank + i // 2, (i % 2) * S:(i % 2 + 1) * S],
                                 weight_part(k, slice(i * P, (i + 1) * P)), act_part(k, slice(0, S)),
                                 k == 0 and i % 2 == 0, k == KC - 1)
                    if k == KC - 1 and i % 2 and i < 2 * FFN_BLOCKS - 1:
                        mm.then_inc(ffn_summed, 1)
                mm.then_inc(weights_used, 1)

            def spread_gain(q):
                pe.matmul(psum[:, 4 + q, :], ones_row[:, :], gain_all[0:1, q * BANK:(q + 1) * BANK], start=True,
                          stop=True).then_inc(gain_spread, 1)

            pe.wait_ge(ones_ready, 1)
            pe.wait_ge(gain_landed[0], 16)
            for q in range(3):
                spread_gain(q)
            pe.wait_ge(ident_ready, 1)
            for b in range(NB):
                norm_turn(0, b)
                if b == 0:
                    spread_gain(3)
                pe.wait_ge(norm_lo_ready, b + 1)
                for k in range(2):
                    pe.wait_ge(lo_ready, k + 1)
                    queries_keys(k, b)
                    mm = value_rows(k, b)
                    if b == NB - 1:
                        mm.then_inc(weights_used, 1)
            norm_turn(0, 2)
            norm_turn(0, 3)
            pe.wait_ge(table_landed, 32)
            pe.matmul(psum[0:MAPS, 3, 0:S], table_sb[:, :], onehot_sb, start=True, stop=True).then_inc(table_summed, 1)
            for k in range(2, KC):
                if k in (4, 5):
                    norm_turn(0, 2 * k - 4)
                    norm_turn(0, 2 * k - 3)
                if k % 4 == 0:
                    pe.wait_ge(norm_lo_ready, (k // 4 + 1) * NB)
                qkv(0, k, first=True)
                if k == CONV_STEP:
                    pe.wait_ge(conv_landed, (TAPS + 1) * 16)
                    pe.wait_ge(table_stored, 1)
                    for t in range(TAPS + 1):
                        mm = turn(psum[:, 3, t * 2 * FC:(t + 1) * 2 * FC], conv_rows[:, t, :], 2 * FC)
                    mm.then_inc(conv_turned, 1)
            with pe.Fori(1, QKV_GROUPS) as g:
                for k in range(KC):
                    qkv(g, k)
                    attention(g - 1, k, QKV_PLAN)
            def o_half(half, step):
                n = half * HEADS + step

                def free(i):
                    if half == 1:
                        pe.wait_ge(oT_stored, HEADS)
                    elif i < NB:
                        pe.wait_ge(qk_stored, NB * QKV_GROUPS - NB + i + 1)
                    elif i == NB:
                        pe.wait_ge(v_stored, QKV_GROUPS)

                project(O_BASE + n, n, step, projection_banks(O_FIRST_BANK[half]), step == 0,
                        step == HEADS - 1, free)

            for h in range(HEADS):
                o_half(0, h)
                attention(QKV_GROUPS - 1, h, O_PLAN)
            for h in range(HEADS):
                o_half(1, h)
            for k in range(KC):
                norm_step(1, k)
                ffn_in(0, k, 0)
            with pe.Fori(0, FFN_GROUPS // 2) as pair:
                for odd in range(2):
                    g = pair * 2 + odd + 1

                    for k in range(KC):
                        ffn_in(g, k, 4 * (1 - odd))
            def out_chunk(half, c, slot, start=False, stop=False):
                def free(i):
                    pe.wait_ge(conv_done, 4 * (FFN_GROUPS - 1 + half))

                project(OUT_BASE + half * FC + c, 2 * HEADS + half * FC + c, slot,
                        projection_banks(OUT_FIRST_BANK[half]), start, stop, free)

            rest = FC % RAW_SLOTS
            for j in range(RAW_SLOTS):
                out_chunk(0, j, j, start=j == 0)
            with pe.Fori(1, FC // RAW_SLOTS) as i:
                for j in range(RAW_SLOTS):
                    out_chunk(0, i * RAW_SLOTS + j, j)
            for j in range(rest):
                out_chunk(0, FC - rest + j, j, stop=j == rest - 1)
            for j in range(rest):
                out_chunk(1, j, rest + j, start=j == 0)
            with pe.Fori(0, FC // RAW_SLOTS - 1) as i:
                for j in range(RAW_SLOTS):
                    out_chunk(1, i * RAW_SLOTS + rest + j, j)
            for j in range(RAW_SLOTS):
                out_chunk(1, FC - RAW_SLOTS + j, j, stop=j == RAW_SLOTS - 1)


INPUTS = ["x", "rel_table", "attn_norm_g", "ffn_norm_g", "da_w_qkv", "da_w_o", "da_q_gain", "da_k_gain",
          "da_lam_q1", "da_lam_k1", "da_lam_q2", "da_lam_k2", "da_sub_gain", "ffn_w_in", "ffn_conv_w",
          "ffn_conv_b", "ffn_w_out"]


def bucket_rows(seq, buckets, max_distance=128):
    import numpy as np

    exact = buckets // 2
    d = np.arange(seq - 1, -1, -1)
    ratio = np.log(np.maximum(d, 1).astype(np.float32) / np.float32(exact)) / np.float32(np.log(max_distance / exact))
    large = np.minimum(exact + (ratio * np.float32(buckets - exact)).astype(np.int32), buckets - 1)
    bucket = np.where(d < exact, d, large)
    return (bucket[None, :] == np.arange(buckets)[:, None]).astype(np.float32)


def kernel(**inputs):
    import numpy as np
    import concourse.bacc as bacc
    from concourse import mybir
    from concourse.bass_utils import run_bass_kernel_spmd

    nc = bacc.Bacc("TRN2", target_bir_lowering=False, num_devices=1)
    arrays = {name: np.ascontiguousarray(inputs[name]) for name in INPUTS}
    arrays["bucket_onehot"] = bucket_rows(inputs["x"].shape[1], inputs["rel_table"].shape[0])
    aps = {name: nc.dram_tensor("in_" + name, a.shape, mybir.dt.from_np(a.dtype), kind="ExternalInput").ap()
           for name, a in arrays.items()}
    out = nc.dram_tensor("result", inputs["x"].shape, mybir.dt.float32, kind="ExternalOutput").ap()
    build_layer(nc, aps["x"], aps["rel_table"], aps["bucket_onehot"], aps["attn_norm_g"], aps["ffn_norm_g"],
                aps["da_w_qkv"], aps["da_w_o"], aps["da_q_gain"], aps["da_k_gain"], aps["da_lam_q1"],
                aps["da_lam_k1"], aps["da_lam_q2"], aps["da_lam_k2"], aps["da_sub_gain"], aps["ffn_w_in"],
                aps["ffn_conv_w"], aps["ffn_conv_b"], aps["ffn_w_out"], out)
    r = run_bass_kernel_spmd(nc, [{"in_" + name: a for name, a in arrays.items()}], core_ids=[0])
    return r.results[0]["result"]
```

```python
from contextlib import ExitStack

import concourse.bass as bass
from concourse import mybir

F32 = mybir.dt.float32
F32R = mybir.dt.float32r
ALU = mybir.AluOpType
ACT = mybir.ActivationFunctionType
AX_X = mybir.AxisListType.X

P = 128
HEAD_DIM = 64
EPS = 1e-6
MASKED = -1e30
LAM_INIT = 0.2
BANK = 512
RAW_SLOTS = 8
SPLIT_SLOTS = 4
SUB = 1024

PE_PARTS = ("turn_qk", "score", "turn_probs", "values", "turn_o")
ACT_PARTS = ("store_qk", "store_qkT", "exps", "store_probsT", "square_o", "store_oT")
DVE_PARTS = ("store_v", "sum_qk", "norm_qk", "bias", "combine", "norm_o")
QKV_PLAN = dict(turn_qk=(4, 5), score=(5, 6), turn_probs=(9, 10), values=(10, 11), turn_o=(12, 13),
                store_qk=(2,), store_qkT=(7, 8), exps=(9, 10), store_probsT=(12, 13), square_o=(13, 14),
                store_oT=(15, 15),
                store_v=(2,), sum_qk=(3,), norm_qk=(5,), bias=(8, 9), combine=(10, 11), norm_o=(13, 14))
O_PLAN = dict(turn_qk=(3, 4), score=(4, 5), turn_probs=(7, 8), values=(8, 9), turn_o=(9, 10),
              store_qk=(1,), store_qkT=(6, 7), exps=(8, 9), store_probsT=(10, 11), square_o=(11, 12),
              store_oT=(12, 13),
              store_v=(1,), sum_qk=(2,), norm_qk=(5,), bias=(7, 8), combine=(9, 10), norm_o=(11, 12))


def run_plan(plan, parts, step, functions):
    for j in range(2):
        for part in parts:
            if j < len(plan[part]) and plan[part][j] == step:
                functions[part](j)


def build_layer(nc, x, rel_table, bucket_onehot, attn_norm_g, ffn_norm_g, w_qkv, w_o, q_gain, k_gain,
                lam_q1, lam_k1, lam_q2, lam_k2, sub_gain, w_in, conv_w, conv_b, w_out, out):
    S, D = x.shape[1], x.shape[2]
    NB = S // P
    KC = D // P
    MAPS = D // HEAD_DIM
    HEADS = MAPS // 2
    VD = 2 * HEAD_DIM
    FF = w_out.shape[1]
    FC = FF // P
    BUCKETS = rel_table.shape[0]
    TAPS = conv_w.shape[1]
    assert (S, D, VD, TAPS) == (2 * P, 2048, P, 3)

    QKV_GROUPS = HEADS // 2
    QW = 2 * VD
    FFN_BLOCKS = 4
    FFN_GROUPS = FC // FFN_BLOCKS
    HALF = D // 2
    O_BASE = QKV_GROUPS * KC
    IN_BASE = O_BASE + 2 * HEADS
    OUT_BASE = IN_BASE + FFN_GROUPS * KC
    assert not (O_BASE % RAW_SLOTS or IN_BASE % RAW_SLOTS or OUT_BASE % RAW_SLOTS or KC % RAW_SLOTS)
    PIECES = KC // 4
    GROUP_RSTD = NB * 8
    TABLE_W = S + P
    BIAS_COPIES = 32
    CONV_STEP = 10

    with ExitStack() as ctx:
        def sb(name, shape, dt=F32):
            return ctx.enter_context(nc.sbuf_tensor(name, shape, dt))

        def sem(name):
            return ctx.enter_context(nc.semaphore(name))

        resid = sb("resid", [P, NB, D])
        act_split = sb("act_split", [P, KC, 2, S], F32R)
        act_hi = act_split[:, :, 0, :]
        act_lo = act_split[:, :, 1, :]
        weight_raw = sb("weight_raw", [P, RAW_SLOTS, SUB])
        weight_hi = sb("weight_hi", [P, SPLIT_SLOTS, SUB], F32R)
        weight_lo = sb("weight_lo", [P, SPLIT_SLOTS, SUB], F32R)
        chunk_hi = sb("chunk_hi", [P, SPLIT_SLOTS, S], F32R)
        chunk_lo = sb("chunk_lo", [P, SPLIT_SLOTS, S], F32R)
        shared = sb("shared", [P, FC * S + D])
        pos_bias = shared[:, 0:MAPS * S].rearrange("p (m k) -> p m k", k=S)
        attn_out = shared[:, MAPS * S:MAPS * S + HEADS * S].rearrange("p (h t) -> p h t", t=S)
        hidden = shared[:, 0:FC * S].rearrange("p (c t) -> p c t", t=S)
        scaled = shared[:, FC * S:FC * S + D]
        work = sb("work", [P, 5120])
        qk = work[:, 0:1024].rearrange("p (b c) -> p b c", b=NB)
        qk_sq = work[:, 1024:2048]
        scores1 = work[:, 1024:2048].rearrange("p (j m k) -> p j m k", j=2, m=2)
        v_sb = work[:, 2048:2560].rearrange("p (b c) -> p b c", b=NB)
        qT = work[:, 2560:3072].rearrange("p (j t) -> p j t", j=2)
        kT = work[:, 3072:3584].rearrange("p (j t) -> p j t", j=2)
        scores0 = work[:, 3584:4096].rearrange("p (j m k) -> p j m k", j=2, m=2)
        probsT = work[:, 4096:4864].rearrange("p (j c q) -> p j c q", j=2, c=3)
        o_junk = work[:, 4864:5120]
        gain_all = work[:, 2048:2048 + D]
        norm_junk = work[:, 4096:5120]
        conv_rows = work[0:2 * FC, 0:(TAPS + 1) * P].rearrange("c (t p) -> c t p", p=P)
        onehot_sb = work[0:BUCKETS, 512:512 + S]
        bias_rows = work[0:MAPS, 768:768 + TABLE_W]
        summed = work[:, 2 * FFN_BLOCKS * S:4 * FFN_BLOCKS * S].rearrange("p (i t) -> p i t", t=S)
        pre_gate = work[:, 0:FFN_BLOCKS * S].rearrange("p (i t) -> p i t", t=S)
        pre_up = work[:, FFN_BLOCKS * S:2 * FFN_BLOCKS * S].rearrange("p (i t) -> p i t", t=S)
        head_out = sb("head_out", [P, 2, NB, VD])
        ident = sb("ident", [P, P])
        ones_row = sb("ones_row", [1, P])
        warm_up = sb("warm_up", [1, 1])
        table_sb = sb("table_sb", [BUCKETS, MAPS])
        conv_cols = sb("conv_cols", [P, TAPS + 1, 2 * FC])
        gains = sb("gains", [P, 5])
        lam_vecs = sb("lam_vecs", [P, 4, HEAD_DIM])
        lam_prod = sb("lam_prod", [P, 2, HEAD_DIM])
        lam_dot = sb("lam_dot", [P, 2])
        lam_exp = sb("lam_exp", [P, 2])
        lam_diff = sb("lam_diff", [P, 1])
        neg_lam = sb("neg_lam", [P, 1])
        norm_sq = sb("norm_sq", [P, NB, 4])
        norm_sum = sb("norm_sum", [P, NB])
        norm_ms = sb("norm_ms", [P, NB])
        norm_rstd = sb("norm_rstd", [P, NB])
        power = sb("power", [P, GROUP_RSTD])
        eps = sb("eps", [P, GROUP_RSTD])
        qk_ss = sb("qk_ss", [P, GROUP_RSTD])
        qk_ms = sb("qk_ms", [P, GROUP_RSTD])
        qk_rstd = sb("qk_rstd", [P, GROUP_RSTD])
        neg_max = sb("neg_max", [P, 2, 4])
        exp_sum = sb("exp_sum", [P, 2, 4])
        coef = sb("coef", [P, 2, 4])
        o_ss = sb("o_ss", [P, 2, NB])
        o_ms = sb("o_ms", [P, 2, NB])
        o_rstd = sb("o_rstd", [P, 2, NB])

        psum = ctx.enter_context(nc.psum_tensor("psum", [P, 8, BANK], F32))
        ps_qkT = psum[:, 4, :]
        ps_o = psum[:, 4, 0:S].rearrange("p (b e) -> p b e", b=NB)
        ps_s1 = psum[:, 5:7, 0:S]
        ps_s0 = psum[:, 5:7, S:S + P]
        ps_pT = psum[:, 7, 0:3 * P].rearrange("p (c q) -> p c q", c=3)
        ps_oT = psum[:, 7, 0:S]
        bias_scratch = nc.dram_tensor("bias_scratch", [MAPS, TABLE_W], F32, kind="Internal").ap()
        bias_copies = nc.dram_tensor("bias_copies", [BIAS_COPIES, MAPS, TABLE_W], F32, kind="Internal").ap()

        raw_landed = [sem(f"raw_landed{i}") for i in range(RAW_SLOTS)]
        hi_ready = sem("hi_ready")
        lo_ready = sem("lo_ready")
        weights_used = sem("weights_used")
        chunk_hi_ready = sem("chunk_hi_ready")
        chunk_lo_ready = sem("chunk_lo_ready")
        x_landed = [sem(f"x_landed{i}") for i in range(2 * NB)]
        gain_landed = [sem("attn_gain_landed"), sem("ffn_gain_landed")]
        small_landed = sem("small_landed")
        conv_landed = sem("conv_landed")
        table_landed = sem("table_landed")
        ones_ready = sem("ones_ready")
        warmed_up = sem("warmed_up")
        gain_spread = sem("gain_spread")
        gain_stored = sem("gain_stored")
        ident_zero = sem("ident_zero")
        ident_ready = sem("ident_ready")
        power_ready = sem("power_ready")
        mask_ready = sem("mask_ready")
        table_summed = sem("table_summed")
        table_stored = sem("table_stored")
        bias_written = sem("bias_written")
        bias_copied = sem("bias_copied")
        bias_landed = sem("bias_landed")
        conv_turned = sem("conv_turned")
        conv_stored = sem("conv_stored")
        gains_step = sem("gains_step")
        lam_step = sem("lam_step")
        lam_exped = sem("lam_exped")
        norm_squared = sem("norm_squared")
        norm_summed = sem("norm_summed")
        norm_ms_ready = sem("norm_ms_ready")
        norm_rstd_ready = sem("norm_rstd_ready")
        norm_scaled = sem("norm_scaled")
        norm_turned = sem("norm_turned")
        norm_hi_ready = sem("norm_hi_ready")
        norm_lo_ready = sem("norm_lo_ready")
        qk_summed = sem("qk_summed")
        qk_stored = sem("qk_stored")
        v_stored = sem("v_stored")
        qk_squared = sem("qk_squared")
        qk_ss_ready = sem("qk_ss_ready")
        qk_ms_ready = sem("qk_ms_ready")
        qk_rstd_ready = sem("qk_rstd_ready")
        qk_normed = sem("qk_normed")
        qk_turned = sem("qk_turned")
        qkT_stored = sem("qkT_stored")
        scores_done = sem("scores_done")
        scores_biased = sem("scores_biased")
        neg_max_ready = sem("neg_max_ready")
        exps_done = sem("exps_done")
        recip_ready = sem("recip_ready")
        coef_ready = sem("coef_ready")
        second_scaled = sem("second_scaled")
        probs_ready = sem("probs_ready")
        probs_turned = sem("probs_turned")
        probsT_stored = sem("probsT_stored")
        values_summed = sem("values_summed")
        o_squared = sem("o_squared")
        o_ms_ready = sem("o_ms_ready")
        o_rstd_ready = sem("o_rstd_ready")
        o_normed = sem("o_normed")
        o_turned = sem("o_turned")
        oT_stored = sem("oT_stored")
        proj_summed = sem("proj_summed")
        resid_added = sem("resid_added")
        ffn_summed = sem("ffn_summed")
        low_copied = sem("low_copied")
        blocks_stored = sem("blocks_stored")
        conv_tap2 = sem("conv_tap2")
        conv_tap1 = sem("conv_tap1")
        conv_done = sem("conv_done")
        gate_ready = sem("gate_ready")
        hidden_ready = sem("hidden_ready")
        out_landed = [sem(f"out_landed{half}") for half in range(2)]

        qkv_rows = w_qkv[0].rearrange("(k p) (s c) -> k p s c", p=P, s=3)
        o_rows = w_o[0].rearrange("(k p) (h c) -> k h p c", p=P, h=2)
        in_rows = w_in[0].rearrange("(k p) (s c) -> k p s c", p=P, s=2)
        out_rows = w_out[0].rearrange("(k p) (h c) -> k h p c", p=P, h=2)
        x_rows = x[0].rearrange("(b p) d -> b p d", p=P)
        result_rows = out[0].rearrange("(b p) d -> b p d", p=P)

        def on_all(vector, n):
            return bass.AP(tensor=vector.tensor, offset=vector.offset, ap=[[0, P], [1, n]])

        def projection_banks(first):
            return [(first + 2 * b + c, b, c) for b in range(NB) for c in range(2)]

        O_FIRST_BANK = (0, 4)
        OUT_FIRST_BANK = (4, 0)

        def ffn_bank(i):
            return (i + FFN_BLOCKS) % (2 * FFN_BLOCKS)

        def piece(q):
            i, b = divmod(q, NB)
            slot = q % 4
            return slice(4 * i, 4 * i + 4), slice(b * P, (b + 1) * P), 4 + slot, slice(slot * BANK, (slot + 1) * BANK)

        def store_half(eng, half):
            for i, (_, b, c) in enumerate(projection_banks(0)):
                eng.wait_ge(resid_added, (2 + half) * 2 * NB + i + 1)
                cols = slice(half * HALF + c * BANK, half * HALF + (c + 1) * BANK)
                eng.dma_start(result_rows[b][:, cols], resid[:, b, cols]).then_inc(out_landed[half], 16)

        block = ctx.enter_context(nc.Block())

        @block.sync
        def _(sp):
            def load(n, slot, dst_cols, src, first=False):
                if not first:
                    sp.wait_ge(lo_ready, n - RAW_SLOTS + 1)
                dst = weight_raw[:, slot, 0:dst_cols]
                if len(src.shape) == 3:
                    dst = dst.rearrange("p (s c) -> p s c", s=src.shape[1])
                sp.dma_start(dst, src).then_inc(raw_landed[slot], 16)

            def load_qkv(g, k, first=False):
                load(g * KC + k, k % RAW_SLOTS, 3 * QW, qkv_rows[k][:, :, bass.ds(g * QW, QW)], first)

            for b in range(NB):
                for i in range(2):
                    cols = slice(i * HALF, (i + 1) * HALF)
                    sp.dma_start(resid[:, b, cols], x_rows[b][:, cols]).then_inc(x_landed[NB * b + i], 16)
            for k in range(RAW_SLOTS):
                load_qkv(0, k, first=True)
            for t in range(TAPS):
                sp.dma_start(conv_rows[:, t, :], conv_w[0, t].rearrange("(c p) -> c p", p=P)).then_inc(conv_landed, 16)
            sp.dma_start(conv_rows[:, TAPS, :], conv_b[0].rearrange("(c p) -> c p", p=P)).then_inc(conv_landed, 16)
            for m in range(2):
                rows = slice(m * HEAD_DIM, (m + 1) * HEAD_DIM)
                sp.dma_start(gains[rows, 0:1], q_gain[0].rearrange("(d a) -> d a", a=1)).then_inc(small_landed, 16)
                sp.dma_start(gains[rows, 1:2], k_gain[0].rearrange("(d a) -> d a", a=1)).then_inc(small_landed, 16)
            sp.dma_start(gains[:, 3:4], sub_gain[0].rearrange("(d a) -> d a", a=1)).then_inc(small_landed, 16)
            for i, vec in enumerate((lam_q1, lam_k1, lam_q2, lam_k2)):
                sp.dma_start(lam_vecs[:, i, :], on_all(vec, HEAD_DIM)).then_inc(small_landed, 16)
            for k in range(RAW_SLOTS, KC):
                load_qkv(0, k)
            with sp.Fori(1, QKV_GROUPS) as g:
                for k in range(KC):
                    load_qkv(g, k)
            for half in range(2):
                with sp.Fori(0, HEADS // RAW_SLOTS) as i:
                    for j in range(RAW_SLOTS):
                        load(O_BASE + half * HEADS + i * RAW_SLOTS + j, j, SUB,
                             o_rows[bass.ds(i * RAW_SLOTS + j, 1), half, :, :].squeeze(0))
                if half == 1:
                    sp.wait_ge(oT_stored, HEADS)
                    sp.dma_start(gain_all, on_all(ffn_norm_g, D)).then_inc(gain_landed[1], 16)
            with sp.Fori(0, FFN_GROUPS) as g:
                for k in range(KC):
                    load(IN_BASE + g * KC + k, k % RAW_SLOTS, SUB, in_rows[k][:, :, bass.ds(g * BANK, BANK)])
            with sp.Fori(0, FC // RAW_SLOTS) as i:
                for j in range(RAW_SLOTS):
                    load(OUT_BASE + i * RAW_SLOTS + j, j, SUB,
                         out_rows[bass.ds(i * RAW_SLOTS + j, 1), 0, :, :].squeeze(0))
            rest = FC % RAW_SLOTS
            for j in range(rest):
                load(OUT_BASE + FC - rest + j, j, SUB, out_rows[FC - rest + j, 0])
            for j in range(rest):
                load(OUT_BASE + FC + j, rest + j, SUB, out_rows[j, 1])
            with sp.Fori(0, FC // RAW_SLOTS) as i:
                for j in range(RAW_SLOTS):
                    load(OUT_BASE + FC + rest + i * RAW_SLOTS + j, j, SUB,
                         out_rows[bass.ds(i * RAW_SLOTS + j + rest, 1), 1, :, :].squeeze(0))
            store_half(sp, 1)
            for half in range(2):
                sp.wait_ge(out_landed[half], 2 * NB * 16)

        @block.gpsimd
        def _(pool):
            pool.memset(ones_row[:, :], 1.0).then_inc(ones_ready, 1)
            pool.memset(ident[:, :], 0.0).then_inc(ident_zero, 1)
            pool.memset(power[:, :], -0.5).then_inc(power_ready, 1)
            pool.memset(eps[:, :], EPS).then_inc(power_ready, 1)
            pool.memset(bias_rows[:, S:TABLE_W], MASKED).then_inc(mask_ready, 1)
            pool.wait_ge(ident_zero, 1)
            pool.affine_select(out=ident[:, :], in_=ident[:, :], compare_op=ALU.not_equal, fill=1.0, base=0,
                               pattern=[[-1, P]], channel_multiplier=1).then_inc(ident_ready, 1)
            pool.wait_ge(power_ready, 2)

            def norm_rstd_step(which, b):
                n = which * NB + b + 1
                pool.wait_ge(norm_summed, n)
                pool.tensor_tensor(norm_ms[:, b:b + 1], norm_sum[:, b:b + 1], eps[:, b:b + 1],
                                   ALU.add).then_inc(norm_ms_ready, 1)
                pool.wait_ge(norm_ms_ready, n)
                pool.tensor_tensor(norm_rstd[:, b:b + 1], norm_ms[:, b:b + 1], power[:, b:b + 1],
                                   ALU.pow).then_inc(norm_rstd_ready, 1)

            def attention_rstds(g):
                pool.wait_ge(qk_ss_ready, g + 1)
                pool.tensor_tensor(qk_ms[:, :], qk_ss[:, :], eps[:, :], ALU.add).then_inc(qk_ms_ready, 1)
                pool.wait_ge(qk_ms_ready, g + 1)
                pool.tensor_tensor(qk_rstd[:, :], qk_ms[:, :], power[:, :], ALU.pow).then_inc(qk_rstd_ready, 1)
                for j in range(2):
                    pool.wait_ge(o_squared, 2 * g + j + 1)
                    pool.tensor_tensor(o_ms[:, j, :], o_ss[:, j, :], eps[:, 0:NB],
                                       ALU.add).then_inc(o_ms_ready, 1)
                    pool.wait_ge(o_ms_ready, 2 * g + j + 1)
                    pool.tensor_tensor(o_rstd[:, j, :], o_ms[:, j, :], power[:, 0:NB],
                                       ALU.pow).then_inc(o_rstd_ready, 1)

            for b in range(NB):
                norm_rstd_step(0, b)
            pool.wait_ge(table_stored, 1)
            pool.wait_ge(mask_ready, 1)
            pool.dma_start(bias_scratch, bias_rows).then_inc(bias_written, 16)
            pool.wait_ge(bias_written, 16)
            pool.dma_start(bias_copies, bass.AP(tensor=bias_scratch.tensor, offset=0,
                                                ap=[[0, BIAS_COPIES], [TABLE_W, MAPS],
                                                    [1, TABLE_W]])).then_inc(bias_copied, 16)
            pool.wait_ge(bias_copied, 16)
            for first in range(0, P, BIAS_COPIES):
                pool.dma_start(pos_bias[first:first + BIAS_COPIES, :, :],
                               bass.AP(tensor=bias_copies.tensor, offset=P - 1 - first,
                                       ap=[[MAPS * TABLE_W - 1, BIAS_COPIES], [TABLE_W, MAPS],
                                           [1, S]])).then_inc(bias_landed, 16)
            with pool.Fori(0, QKV_GROUPS) as g:
                attention_rstds(g)
            for b in range(NB):
                norm_rstd_step(1, b)
            store_half(pool, 0)

        @block.scalar
        def _(act):
            act.dma_start(gain_all[0:1, :], attn_norm_g).then_inc(gain_landed[0], 16)
            act.wait_ge(ones_ready, 1)
            act.activation(warm_up[:, :], ones_row[:, 0:1], ACT.Square).then_inc(warmed_up, 1)
            act.dma_start(table_sb[:, :], rel_table).then_inc(table_landed, 16)
            act.dma_start(onehot_sb, bucket_onehot).then_inc(table_landed, 16)

            def split_weights(n, slot, cols):
                act.wait_ge(raw_landed[slot % RAW_SLOTS], (n - slot % RAW_SLOTS) * (16 // RAW_SLOTS) + 16)
                if not (isinstance(n, int) and n < SPLIT_SLOTS):
                    act.wait_ge(weights_used, n - SPLIT_SLOTS + 1)
                act.activation(weight_hi[:, slot % SPLIT_SLOTS, 0:cols], weight_raw[:, slot % RAW_SLOTS, 0:cols],
                               ACT.Copy).then_inc(hi_ready, 1)

            def split_chunk(slot, src):
                act.activation(chunk_hi[:, slot % SPLIT_SLOTS, :], src, ACT.Copy).then_inc(chunk_hi_ready, 1)

            def norm_squares(n, b, piece, cols):
                if n:
                    act.wait_ge(norm_squared, n)
                act.activation(norm_junk[:, 0:cols.stop - cols.start], resid[:, b, cols], ACT.Square, scale=D ** -0.5,
                               accum_out=norm_sq[:, b, piece:piece + 1]).then_inc(norm_squared, 1)

            def norm_hi(which, q):
                chunks, tokens, bank, _ = piece(q)
                act.wait_ge(norm_turned, which * NB * PIECES + q + 1)
                act.activation(act_hi[:, chunks, tokens], psum[:, bank, :].rearrange("p (c t) -> p c t", t=P),
                               ACT.Copy).then_inc(norm_hi_ready, 1)

            def norm_rest(which, base, cols):
                for k in (4, 5):
                    split_weights(base + k, k, cols)
                    norm_hi(which, 2 * k - 4)
                    norm_hi(which, 2 * k - 3)

            def attention(g, step, plan):
                def store_qk(_):
                    for b in range(NB):
                        act.wait_ge(qk_summed, NB * g + b + 1)
                        act.activation(qk[:, b, :], psum[:, b, :], ACT.Copy).then_inc(qk_stored, 1)
                    act.wait_ge(qk_stored, NB * g + NB)
                    act.activation(qk_sq, qk.rearrange("p b c -> p (b c)"), ACT.Square,
                                   scale=HEAD_DIM ** -0.5).then_inc(qk_squared, 1)

                def store_qkT(j):
                    act.wait_ge(qk_turned, 2 * g + j + 1)
                    act.activation(qT[:, j, :], ps_qkT[:, 0:S], ACT.Copy, scale=gains[:, 2:3])
                    act.activation(kT[:, j, :], ps_qkT[:, S:2 * S], ACT.Copy).then_inc(qkT_stored, 1)

                def exps(j):
                    act.wait_ge(neg_max_ready, 2 * g + j + 1)
                    for m in range(2):
                        act.activation(scores1[:, j, m, :], scores1[:, j, m, :], ACT.Exp,
                                       bias=neg_max[:, j, 2 + m:3 + m], accum_out=exp_sum[:, j, 2 + m:3 + m])
                    for m in range(2):
                        ins = act.activation(scores0[:, j, m, :], scores0[:, j, m, :], ACT.Exp,
                                             bias=neg_max[:, j, m:m + 1], accum_out=exp_sum[:, j, m:m + 1])
                    ins.then_inc(exps_done, 1)

                def store_probsT(j):
                    act.wait_ge(probs_turned, 2 * g + j + 1)
                    act.activation(probsT[:, j, :, :], ps_pT, ACT.Copy).then_inc(probsT_stored, 1)

                def square_o(j):
                    act.wait_ge(values_summed, 2 * g + j + 1)
                    for b in range(NB):
                        ins = act.activation(o_junk[:, b * VD:(b + 1) * VD], ps_o[:, b, :], ACT.Square, scale=VD ** -0.5,
                                             accum_out=o_ss[:, j, b:b + 1])
                    ins.then_inc(o_squared, 1)

                def store_oT(j):
                    act.wait_ge(o_turned, 2 * g + j + 1)
                    act.activation(attn_out[:, bass.ds(2 * g + j, 1), :].squeeze(1), ps_oT, ACT.Copy,
                                   scale=gains[:, 4:5]).then_inc(oT_stored, 1)

                run_plan(plan, ACT_PARTS, step, dict(store_qk=store_qk, store_qkT=store_qkT, exps=exps,
                                                     store_probsT=store_probsT, square_o=square_o,
                                                     store_oT=store_oT))

            def copy_low(g):
                for i in range(2 * FFN_BLOCKS):
                    if i < 2 * FFN_BLOCKS - 1:
                        act.wait_ge(ffn_summed, FFN_BLOCKS - 1 + (g - 1) * (2 * FFN_BLOCKS - 1) + i + 1)
                    else:
                        act.wait_ge(weights_used, IN_BASE + (g + 1) * KC)
                    if i == 0:
                        act.wait_ge(hidden_ready, g)
                    dst = (pre_gate if i < FFN_BLOCKS else pre_up)[:, i % FFN_BLOCKS, :]
                    act.activation(dst, psum[:, ffn_bank(i), S:2 * S], ACT.Copy).then_inc(low_copied, 1)

            def convolve(g, pair):
                act.wait_ge(blocks_stored, 2 * FFN_BLOCKS * g + 2 * pair + 2)
                for i in (2 * pair, 2 * pair + 1):
                    col = (FC if i >= FFN_BLOCKS else 0) + g * FFN_BLOCKS + i % FFN_BLOCKS
                    dst = (pre_gate if i < FFN_BLOCKS else pre_up)[:, i % FFN_BLOCKS, :]
                    ins = act.activation(dst, summed[:, i, :], ACT.Identity,
                                         bias=conv_cols[:, TAPS, bass.ds(col, 1)],
                                         scale=conv_cols[:, TAPS - 1, bass.ds(col, 1)])
                ins.then_inc(conv_tap2, 1)

            def hidden_step(g, step, first=False):
                if step == 1 and not first:
                    copy_low(g)
                if 2 <= step < 6:
                    convolve(g, step - 2)
                if step == 6:
                    act.wait_ge(conv_done, 4 * g + 2)
                    act.activation(pre_gate, pre_gate, ACT.Silu).then_inc(gate_ready, 1)

            for b in range(NB):
                for i in range(2):
                    act.wait_ge(x_landed[NB * b + i], 16)
                    norm_squares(NB * b + i, b, i, slice(i * HALF, (i + 1) * HALF))
            norm_hi(0, 0)
            split_weights(0, 0, 3 * QW)
            split_weights(1, 1, 3 * QW)
            norm_hi(0, 1)
            split_weights(2, 2, 3 * QW)
            norm_hi(0, 2)
            norm_hi(0, 3)
            split_weights(3, 3, 3 * QW)
            norm_rest(0, 0, 3 * QW)
            for k in range(6, KC):
                split_weights(k, k, 3 * QW)
                if k == CONV_STEP + 3:
                    act.wait_ge(conv_turned, 1)
                    act.activation(conv_cols[:, :, :],
                                   psum[:, 3, 0:(TAPS + 1) * 2 * FC].rearrange("p (t c) -> p t c", c=2 * FC),
                                   ACT.Copy).then_inc(conv_stored, 1)
            act.wait_ge(lam_step, 2)
            act.activation(lam_exp[:, :], lam_dot[:, :], ACT.Exp).then_inc(lam_exped, 1)
            act.wait_ge(bias_written, 16)
            with act.Fori(1, QKV_GROUPS) as g:
                for k in range(KC):
                    split_weights(g * KC + k, k, 3 * QW)
                    attention(g - 1, k, QKV_PLAN)
            for h in range(HEADS):
                split_weights(O_BASE + h, h, SUB)
                if h >= HEADS - 2:
                    act.wait_ge(oT_stored, h + 1)
                split_chunk(h, attn_out[:, h, :])
                attention(QKV_GROUPS - 1, h, O_PLAN)
            for h in range(HEADS):
                split_weights(O_BASE + HEADS + h, h, SUB)
                split_chunk(h, attn_out[:, h, :])
                if 4 <= h < 4 + 2 * NB:
                    i = h - 4
                    act.wait_ge(resid_added, i + 1)
                    norm_squares(4 + i, i // 2, i % 2, slice((i % 2) * BANK, (i % 2 + 1) * BANK))
            for n in range(2):
                split_weights(IN_BASE + n, n, SUB)
            for i in range(2 * NB):
                act.wait_ge(resid_added, 2 * NB + i + 1)
                norm_squares(8 + i, i // 2, 2 + i % 2, slice(HALF + (i % 2) * BANK, HALF + (i % 2 + 1) * BANK))
            norm_hi(1, 0)
            norm_hi(1, 1)
            split_weights(IN_BASE + 2, 2, SUB)
            norm_hi(1, 2)
            norm_hi(1, 3)
            split_weights(IN_BASE + 3, 3, SUB)
            norm_rest(1, IN_BASE, SUB)
            for k in range(6, KC):
                split_weights(IN_BASE + k, k, SUB)
            for k in range(KC):
                split_weights(IN_BASE + KC + k, k, SUB)
                hidden_step(0, k, first=True)
            with act.Fori(2, FFN_GROUPS) as g:
                for k in range(KC):
                    split_weights(IN_BASE + g * KC + k, k, SUB)
                    hidden_step(g - 1, k)
            for j in range(RAW_SLOTS):
                split_weights(OUT_BASE + j, j, SUB)
                split_chunk(j, hidden[:, j, :])
                hidden_step(FFN_GROUPS - 1, j)
            with act.Fori(1, FC // RAW_SLOTS) as i:
                for j in range(RAW_SLOTS):
                    split_weights(OUT_BASE + i * RAW_SLOTS + j, j, SUB)
                    split_chunk(j, hidden[:, bass.ds(i * RAW_SLOTS + j, 1), :].squeeze(1))
            rest = FC % RAW_SLOTS
            for j in range(rest):
                split_weights(OUT_BASE + FC - rest + j, j, SUB)
                if j == 0:
                    act.wait_ge(hidden_ready, FFN_GROUPS)
                split_chunk(j, hidden[:, FC - rest + j, :])
            for j in range(rest):
                split_weights(OUT_BASE + FC + j, rest + j, SUB)
                split_chunk(rest + j, hidden[:, j, :])
            with act.Fori(0, FC // RAW_SLOTS) as i:
                for j in range(RAW_SLOTS):
                    split_weights(OUT_BASE + FC + rest + i * RAW_SLOTS + j, j, SUB)
                    split_chunk(j, hidden[:, bass.ds(i * RAW_SLOTS + j + rest, 1), :].squeeze(1))

        @block.vector
        def _(dve):
            def split_weights(n, slot, cols):
                dve.wait_ge(hi_ready, n + 1)
                dve.tensor_tensor(weight_lo[:, slot % SPLIT_SLOTS, 0:cols], weight_raw[:, slot % RAW_SLOTS, 0:cols],
                                  weight_hi[:, slot % SPLIT_SLOTS, 0:cols].bitcast(F32),
                                  ALU.subtract).then_inc(lo_ready, 1)

            def split_chunk(m, slot, src):
                dve.wait_ge(chunk_hi_ready, m + 1)
                dve.tensor_tensor(chunk_lo[:, slot % SPLIT_SLOTS, :], src,
                                  chunk_hi[:, slot % SPLIT_SLOTS, :].bitcast(F32),
                                  ALU.subtract).then_inc(chunk_lo_ready, 1)

            def norm_total(which, b, pieces):
                dve.wait_ge(norm_squared, 2 * NB + 2 * NB + 2 * (b + 1) if which else 2 * (b + 1))
                dve.tensor_reduce(norm_sum[:, b:b + 1], norm_sq[:, b, 0:pieces], AX_X, ALU.add).then_inc(norm_summed, 1)

            def norm_scale(which, q):
                (i, b), n = divmod(q, NB), which * NB * PIECES + q
                dve.wait_ge(norm_rstd_ready, which * NB + b + 1)
                if q >= 4:
                    dve.wait_ge(norm_turned, n - 3)
                cols = slice(i * BANK, (i + 1) * BANK)
                dve.scalar_tensor_tensor(out=scaled[:, piece(q)[3]], in0=resid[:, b, cols],
                                         scalar=norm_rstd[:, b:b + 1], in1=gain_all[:, cols],
                                         op0=ALU.mult, op1=ALU.mult).then_inc(norm_scaled, 1)

            def norm_lo(which, q):
                chunks, tokens, bank, _ = piece(q)
                dve.wait_ge(norm_hi_ready, which * NB * PIECES + q + 1)
                dve.tensor_tensor(act_lo[:, chunks, tokens], psum[:, bank, :].rearrange("p (c t) -> p c t", t=P),
                                  act_hi[:, chunks, tokens].bitcast(F32), ALU.subtract).then_inc(norm_lo_ready, 1)

            def norm_rest(which, base, cols):
                for k in (4, 5):
                    for q in (2 * k - 4, 2 * k - 3):
                        norm_scale(which, q)
                    split_weights(base + k, k, cols)
                    for q in (2 * k - 4, 2 * k - 3):
                        norm_lo(which, q)

            def attention(g, step, plan):
                def store_v(_):
                    dve.wait_ge(weights_used, (g + 1) * KC)
                    dve.tensor_copy(v_sb, psum[:, NB, :].rearrange("p (b c) -> p b c", b=NB)).then_inc(v_stored, 1)

                def sum_qk(_):
                    dve.wait_ge(qk_squared, g + 1)
                    dve.tensor_reduce(qk_ss[:, :], qk_sq.rearrange("p (m d) -> p m d", d=HEAD_DIM), AX_X,
                                      ALU.add).then_inc(qk_ss_ready, 1)

                def norm_qk(_):
                    dve.wait_ge(qk_rstd_ready, g + 1)
                    rows = qk.rearrange("p b (m d) -> p (b m) d", d=HEAD_DIM)
                    dve.tensor_tensor(rows, rows, qk_rstd[:, :].unsqueeze(2).to_broadcast([P, GROUP_RSTD, HEAD_DIM]),
                                      ALU.mult).then_inc(qk_normed, 1)

                def bias(j):
                    n = 2 * g + j + 1
                    dve.wait_ge(bias_landed, P // BIAS_COPIES * 16)
                    dve.wait_ge(scores_done, n)
                    maps = bass.ds(4 * g + 2 * j, 2)
                    dve.tensor_tensor(scores1[:, j, :, :], ps_s1, pos_bias[:, maps, :], ALU.add)
                    dve.tensor_tensor(scores0[:, j, :, :], ps_s0, pos_bias[:, maps, P:S],
                                      ALU.add).then_inc(scores_biased, 1)
                    dve.wait_ge(scores_biased, n)
                    dve.tensor_reduce(neg_max[:, j, 2:4], scores1[:, j, :, :], AX_X, ALU.max, negate=True)
                    dve.tensor_reduce(neg_max[:, j, 0:2], scores0[:, j, :, :], AX_X, ALU.max,
                                      negate=True).then_inc(neg_max_ready, 1)

                def combine(j):
                    n = 2 * g + j + 1
                    dve.wait_ge(exps_done, n)
                    dve.reciprocal(coef[:, j, :], exp_sum[:, j, :]).then_inc(recip_ready, 1)
                    dve.wait_ge(recip_ready, n)
                    second = coef[:, j, :].rearrange("p (b m) -> p b m", m=2)[:, :, 1]
                    dve.tensor_scalar(second, second, neg_lam[:, :], None, ALU.mult).then_inc(coef_ready, 1)
                    dve.wait_ge(coef_ready, n)
                    dve.tensor_scalar(scores1[:, j, 1, :], scores1[:, j, 1, :], coef[:, j, 3:4], None, ALU.mult)
                    dve.tensor_scalar(scores0[:, j, 1, :], scores0[:, j, 1, :], coef[:, j, 1:2], None,
                                      ALU.mult).then_inc(second_scaled, 1)
                    dve.wait_ge(second_scaled, n)
                    dve.scalar_tensor_tensor(out=scores1[:, j, 0, :], in0=scores1[:, j, 0, :],
                                             scalar=coef[:, j, 2:3], in1=scores1[:, j, 1, :],
                                             op0=ALU.mult, op1=ALU.add)
                    dve.scalar_tensor_tensor(out=scores0[:, j, 0, :], in0=scores0[:, j, 0, :],
                                             scalar=coef[:, j, 0:1], in1=scores0[:, j, 1, :],
                                             op0=ALU.mult, op1=ALU.add).then_inc(probs_ready, 1)

                def norm_o(j):
                    dve.wait_ge(o_rstd_ready, 2 * g + j + 1)
                    dve.tensor_tensor(head_out[:, j, :, :], ps_o,
                                      o_rstd[:, j, :].unsqueeze(2).to_broadcast([P, NB, VD]),
                                      ALU.mult).then_inc(o_normed, 1)

                run_plan(plan, DVE_PARTS, step, dict(store_v=store_v, sum_qk=sum_qk, norm_qk=norm_qk, bias=bias,
                                                     combine=combine, norm_o=norm_o))

            def store_blocks(g, first=False):
                if first:
                    for bank in range(FFN_BLOCKS):
                        if bank < FFN_BLOCKS - 1:
                            dve.wait_ge(ffn_summed, bank + 1)
                        else:
                            dve.wait_ge(weights_used, IN_BASE + KC)
                        dve.tensor_copy(summed[:, 2 * bank:2 * bank + 2, :],
                                        psum[:, bank, :].rearrange("p (i t) -> p i t", t=S)).then_inc(blocks_stored, 2)
                    return
                for i in range(2 * FFN_BLOCKS):
                    low = (pre_gate if i < FFN_BLOCKS else pre_up)[:, i % FFN_BLOCKS, :]
                    dve.wait_ge(low_copied, (g - 1) * 2 * FFN_BLOCKS + i + 1)
                    dve.tensor_tensor(summed[:, i, :], psum[:, ffn_bank(i), 0:S], low, ALU.add).then_inc(blocks_stored, 1)

            def convolve(g, pair):
                n = 4 * g + pair + 1
                dve.wait_ge(conv_tap2, n)
                dve.wait_ge(blocks_stored, 2 * FFN_BLOCKS * g + 2 * pair + 2)
                for tap in range(TAPS - 2, -1, -1):
                    shift = TAPS - 1 - tap
                    for i in (2 * pair, 2 * pair + 1):
                        col = (FC if i >= FFN_BLOCKS else 0) + g * FFN_BLOCKS + i % FFN_BLOCKS
                        dst = (pre_gate if i < FFN_BLOCKS else pre_up)[:, i % FFN_BLOCKS, shift:S]
                        ins = dve.scalar_tensor_tensor(
                            out=dst, in0=summed[:, i, 0:S - shift],
                            scalar=conv_cols[:, tap, bass.ds(col, 1)], in1=dst, op0=ALU.mult, op1=ALU.add)
                    ins.then_inc(conv_done if tap == 0 else conv_tap1, 1)
                    if tap:
                        dve.wait_ge(conv_tap1, n)

            def hidden_step(g, step, steps, first=False):
                if step == 1:
                    store_blocks(g, first)
                if step in steps[0:4]:
                    convolve(g, steps.index(step))
                if step == steps[4]:
                    dve.wait_ge(gate_ready, g + 1)
                    dve.wait_ge(conv_done, 4 * g + 4)
                    dve.tensor_tensor(hidden[:, bass.ds(g * FFN_BLOCKS, FFN_BLOCKS), :], pre_gate, pre_up,
                                      ALU.mult).then_inc(hidden_ready, 1)

            def add_residual(half, i, first_bank, stage, used):
                bank, b, c = projection_banks(first_bank)[i]
                cols = slice(half * HALF + c * BANK, half * HALF + (c + 1) * BANK)
                if i < 2 * NB - 1:
                    dve.wait_ge(proj_summed, (2 * stage + half) * (2 * NB - 1) + i + 1)
                else:
                    dve.wait_ge(weights_used, used)
                dve.tensor_tensor(resid[:, b, cols], psum[:, bank, :], resid[:, b, cols],
                                  ALU.add).then_inc(resid_added, 1)

            def store_gain(q):
                dve.wait_ge(gain_spread, q + 1)
                dve.tensor_copy(gain_all[:, q * BANK:(q + 1) * BANK], psum[:, 4 + q, :]).then_inc(gain_stored, 1)

            def scale_first(q):
                dve.wait_ge(gain_stored, q // NB + 1)
                norm_scale(0, q)

            norm_total(0, 0, 2)
            store_gain(0)
            scale_first(0)
            store_gain(1)
            norm_total(0, 1, 2)
            norm_lo(0, 0)
            split_weights(0, 0, 3 * QW)
            scale_first(1)
            split_weights(1, 1, 3 * QW)
            store_gain(2)
            norm_lo(0, 1)
            scale_first(2)
            store_gain(3)
            split_weights(2, 2, 3 * QW)
            scale_first(3)
            norm_lo(0, 2)
            split_weights(3, 3, 3 * QW)
            norm_lo(0, 3)
            dve.wait_ge(table_summed, 1)
            dve.tensor_copy(bias_rows[:, 0:S], psum[0:MAPS, 3, 0:S]).then_inc(table_stored, 1)
            dve.wait_ge(gain_stored, 4)
            norm_rest(0, 0, 3 * QW)
            for k in range(6, KC):
                split_weights(k, k, 3 * QW)
            dve.wait_ge(small_landed, 9 * 16)
            dve.tensor_tensor(gains[:, 2:3], gains[:, 0:1], gains[:, 1:2], ALU.mult).then_inc(gains_step, 1)
            dve.tensor_scalar(gains[:, 4:5], gains[:, 3:4], 1.0 - LAM_INIT, None, ALU.mult).then_inc(gains_step, 1)
            lam_pairs = lam_vecs[:, :, :].rearrange("p (i s) d -> p i s d", s=2)
            dve.tensor_tensor(lam_prod[:, :, :], lam_pairs[:, :, 0, :], lam_pairs[:, :, 1, :],
                              ALU.mult).then_inc(lam_step, 1)
            dve.wait_ge(gains_step, 2)
            dve.tensor_scalar(gains[:, 2:3], gains[:, 2:3], HEAD_DIM ** -0.5, None, ALU.mult).then_inc(gains_step, 1)
            dve.wait_ge(lam_step, 1)
            dve.tensor_reduce(lam_dot[:, :], lam_prod[:, :, :], AX_X, ALU.add).then_inc(lam_step, 1)
            dve.wait_ge(lam_exped, 1)
            dve.tensor_tensor(lam_diff[:, :], lam_exp[:, 1:2], lam_exp[:, 0:1], ALU.subtract).then_inc(lam_step, 1)
            dve.wait_ge(lam_step, 3)
            dve.tensor_scalar(neg_lam[:, :], lam_diff[:, :], LAM_INIT, None, ALU.subtract).then_inc(lam_step, 1)
            dve.wait_ge(lam_step, 4)
            with dve.Fori(1, QKV_GROUPS) as g:
                for k in range(KC):
                    split_weights(g * KC + k, k, 3 * QW)
                    attention(g - 1, k, QKV_PLAN)
            for h in range(HEADS):
                split_weights(O_BASE + h, h, SUB)
                split_chunk(h, h, attn_out[:, h, :])
                attention(QKV_GROUPS - 1, h, O_PLAN)
            for h in range(HEADS):
                split_weights(O_BASE + HEADS + h, h, SUB)
                split_chunk(HEADS + h, h, attn_out[:, h, :])
                if 3 <= h < 3 + 2 * NB:
                    add_residual(0, h - 3, O_FIRST_BANK[0], 0, O_BASE + HEADS)
            for n in range(2):
                split_weights(IN_BASE + n, n, SUB)
            for i in range(2 * NB - 1):
                add_residual(1, i, O_FIRST_BANK[1], 0, IN_BASE)
            norm_total(1, 0, 4)
            add_residual(1, 2 * NB - 1, O_FIRST_BANK[1], 0, IN_BASE)
            dve.wait_ge(gain_landed[1], 16)
            norm_scale(1, 0)
            norm_total(1, 1, 4)
            norm_scale(1, 1)
            norm_lo(1, 0)
            norm_scale(1, 2)
            norm_lo(1, 1)
            split_weights(IN_BASE + 2, 2, SUB)
            norm_scale(1, 3)
            norm_lo(1, 2)
            norm_lo(1, 3)
            split_weights(IN_BASE + 3, 3, SUB)
            norm_rest(1, IN_BASE, SUB)
            for k in range(6, KC):
                split_weights(IN_BASE + k, k, SUB)
            for k in range(KC):
                split_weights(IN_BASE + KC + k, k, SUB)
                hidden_step(0, k, (3, 5, 7, 9, 10), first=True)
            with dve.Fori(2, FFN_GROUPS) as g:
                for k in range(KC):
                    split_weights(IN_BASE + g * KC + k, k, SUB)
                    hidden_step(g - 1, k, (3, 5, 7, 9, 10))
            for j in range(RAW_SLOTS):
                split_weights(OUT_BASE + j, j, SUB)
                split_chunk(2 * HEADS + j, j, hidden[:, j, :])
                hidden_step(FFN_GROUPS - 1, j, (3, 4, 5, 6, 7))
            with dve.Fori(1, FC // RAW_SLOTS) as i:
                for j in range(RAW_SLOTS):
                    split_weights(OUT_BASE + i * RAW_SLOTS + j, j, SUB)
                    split_chunk(2 * HEADS + i * RAW_SLOTS + j, j, hidden[:, bass.ds(i * RAW_SLOTS + j, 1), :].squeeze(1))
            rest = FC % RAW_SLOTS
            for j in range(rest):
                split_weights(OUT_BASE + FC - rest + j, j, SUB)
                split_chunk(2 * HEADS + FC - rest + j, j, hidden[:, FC - rest + j, :])
            for j in range(rest):
                split_weights(OUT_BASE + FC + j, rest + j, SUB)
                split_chunk(2 * HEADS + FC + j, rest + j, hidden[:, j, :])
                if j >= rest - 2:
                    for i in range(NB):
                        add_residual(0, NB * (j - rest + 2) + i, OUT_FIRST_BANK[0], 1, OUT_BASE + FC)
            with dve.Fori(0, FC // RAW_SLOTS) as i:
                for j in range(RAW_SLOTS):
                    split_weights(OUT_BASE + FC + rest + i * RAW_SLOTS + j, j, SUB)
                    split_chunk(2 * HEADS + FC + rest + i * RAW_SLOTS + j, j,
                                hidden[:, bass.ds(i * RAW_SLOTS + j + rest, 1), :].squeeze(1))
            for i in range(2 * NB):
                add_residual(1, i, OUT_FIRST_BANK[1], 1, OUT_BASE + 2 * FC)

        @block.tensor
        def _(pe):
            def product(dst, left, right, start, stop):
                (left_hi, left_lo), (right_hi, right_lo) = left, right
                pe.matmul(dst, left_hi, right_hi, start=start, stop=False, skip_group_check=True)
                pe.matmul(dst, left_hi, right_lo, start=False, stop=False, skip_group_check=True)
                return pe.matmul(dst, left_lo, right_hi, start=False, stop=stop, skip_group_check=True)

            def act_part(k, tokens):
                return act_hi[:, k, tokens], act_lo[:, k, tokens]

            def weight_part(slot, cols):
                return weight_hi[:, slot % SPLIT_SLOTS, cols], weight_lo[:, slot % SPLIT_SLOTS, cols]

            def queries_keys(k, b):
                return product(psum[:, b, :], act_part(k, slice(b * P, (b + 1) * P)),
                               weight_part(k, slice(0, 2 * QW)), k == 0, k == KC - 1)

            def value_rows(k, b):
                return product(psum[:, NB, b * QW:(b + 1) * QW], act_part(k, slice(b * P, (b + 1) * P)),
                               weight_part(k, slice(2 * QW, 3 * QW)), k == 0 and b == 0, k == KC - 1)

            def qkv(g, k, first=False):
                pe.wait_ge(lo_ready, g * KC + k + 1)
                for b in range(NB):
                    if k == 0 and not first:
                        pe.wait_ge(qk_stored, NB * (g - 1) + b + 1)
                    mm = queries_keys(k, b)
                    if k == KC - 1:
                        mm.then_inc(qk_summed, 1)
                if k == 0 and not first:
                    pe.wait_ge(v_stored, g)
                for b in range(NB):
                    mm = value_rows(k, b)
                mm.then_inc(weights_used, 1)

            def norm_turn(which, q):
                _, _, bank, cols = piece(q)
                n = which * NB * PIECES + q
                pe.wait_ge(norm_scaled, n + 1)
                if q >= 4:
                    pe.wait_ge(norm_lo_ready, n - 3)
                for c in range(4):
                    mm = turn(psum[:, bank, c * P:(c + 1) * P], scaled[:, cols][:, c * P:(c + 1) * P])
                mm.then_inc(norm_turned, 1)

            def norm_rest(which, k):
                if k in (4, 5):
                    norm_turn(which, 2 * k - 4)
                    norm_turn(which, 2 * k - 3)
                if k % 4 == 0:
                    pe.wait_ge(norm_lo_ready, (which * PIECES + k // 4 + 1) * NB)

            def turn(dst, src, k=P):
                return pe.transpose(dst, src, ident[0:k, 0:k])

            def attention(g, step, plan):
                def turn_qk(j):
                    pe.wait_ge(qk_normed, g + 1)
                    if j == 1:
                        pe.wait_ge(qkT_stored, 2 * g + 1)
                    for part in range(2):
                        for b in range(NB):
                            cols = slice(part * QW + j * VD, part * QW + (j + 1) * VD)
                            mm = turn(ps_qkT[:, part * S + b * P:part * S + (b + 1) * P], qk[:, b, cols])
                    mm.then_inc(qk_turned, 1)

                def score(j):
                    pe.wait_ge(qkT_stored, 2 * g + j + 1)
                    if j == 1:
                        pe.wait_ge(scores_biased, 2 * g + 1)
                    for m in range(2):
                        rows = slice(m * HEAD_DIM, (m + 1) * HEAD_DIM)
                        pe.matmul(ps_s1[:, m, :], qT[rows, j, P:S], kT[rows, j, :], start=True, stop=True)
                    for m in range(2):
                        rows = slice(m * HEAD_DIM, (m + 1) * HEAD_DIM)
                        mm = pe.matmul(ps_s0[:, m, :], qT[rows, j, 0:P], kT[rows, j, 0:P], start=True, stop=True)
                    mm.then_inc(scores_done, 1)

                def turn_probs(j):
                    pe.wait_ge(probs_ready, 2 * g + j + 1)
                    if j == 1:
                        pe.wait_ge(probsT_stored, 2 * g + 1)
                    for c in range(NB):
                        turn(ps_pT[:, c, :], scores1[:, j, 0, c * P:(c + 1) * P])
                    turn(ps_pT[:, NB, :], scores0[:, j, 0, :]).then_inc(probs_turned, 1)

                def values(j):
                    pe.wait_ge(probsT_stored, 2 * g + j + 1)
                    if j == 0:
                        pe.wait_ge(qkT_stored, 2 * g + 2)
                    else:
                        pe.wait_ge(o_normed, 2 * g + 1)
                    cols = slice(j * VD, (j + 1) * VD)
                    pe.matmul(ps_o[:, 0, :], probsT[:, j, NB, :], v_sb[:, 0, cols], start=True, stop=True)
                    pe.matmul(ps_o[:, 1, :], probsT[:, j, 0, :], v_sb[:, 0, cols], start=True, stop=False)
                    pe.matmul(ps_o[:, 1, :], probsT[:, j, 1, :], v_sb[:, 1, cols], start=False,
                              stop=True).then_inc(values_summed, 1)

                def turn_o(j):
                    pe.wait_ge(o_normed, 2 * g + j + 1)
                    if j == 0:
                        pe.wait_ge(probsT_stored, 2 * g + 2)
                    else:
                        pe.wait_ge(oT_stored, 2 * g + 1)
                    turn(ps_oT[:, 0:P], head_out[:, j, 0, :])
                    turn(ps_oT[:, P:S], head_out[:, j, 1, :]).then_inc(o_turned, 1)

                run_plan(plan, PE_PARTS, step, dict(turn_qk=turn_qk, score=score, turn_probs=turn_probs,
                                                    values=values, turn_o=turn_o))

            def project(n, m, slot, banks, start=False, stop=False, free=None):
                pe.wait_ge(lo_ready, n + 1)
                pe.wait_ge(chunk_lo_ready, m + 1)
                for i, (bank, b, c) in enumerate(banks):
                    if start:
                        free(bank)
                    tokens = slice(b * P, (b + 1) * P)
                    s = slot % SPLIT_SLOTS
                    mm = product(psum[:, bank, :], (chunk_hi[:, s, tokens], chunk_lo[:, s, tokens]),
                                 weight_part(slot, slice(c * BANK, (c + 1) * BANK)), start, stop)
                    if stop and i < 2 * NB - 1:
                        mm.then_inc(proj_summed, 1)
                mm.then_inc(weights_used, 1)

            def ffn_in_first(k):
                pe.wait_ge(lo_ready, IN_BASE + k + 1)
                for i in range(2 * FFN_BLOCKS):
                    mm = product(psum[:, i // 2, (i % 2) * S:(i % 2 + 1) * S],
                                 weight_part(k, slice(i * P, (i + 1) * P)), act_part(k, slice(0, S)),
                                 k == 0 and i % 2 == 0, k == KC - 1)
                    if k == KC - 1 and i % 2 and i < 2 * FFN_BLOCKS - 1:
                        mm.then_inc(ffn_summed, 1)
                mm.then_inc(weights_used, 1)

            def ffn_in(g, k):
                pe.wait_ge(lo_ready, IN_BASE + g * KC + k + 1)
                for i in range(2 * FFN_BLOCKS):
                    if k == 0:
                        pe.wait_ge(blocks_stored, 2 * FFN_BLOCKS * (g - 1) + i + 1)
                    w_hi, w_lo = weight_part(k, slice(i * P, (i + 1) * P))
                    pe.matmul(psum[:, ffn_bank(i), :], w_hi, act_split[:, k, :, :].rearrange("p s t -> p (s t)"),
                              start=k == 0, stop=k == KC - 1, skip_group_check=True)
                    mm = pe.matmul(psum[:, ffn_bank(i), 0:S], w_lo, act_hi[:, k, :], start=False,
                                   stop=k == KC - 1, skip_group_check=True)
                    if k == KC - 1 and i < 2 * FFN_BLOCKS - 1:
                        mm.then_inc(ffn_summed, 1)
                mm.then_inc(weights_used, 1)

            def spread_gain(q):
                pe.matmul(psum[:, 4 + q, :], ones_row[:, :], gain_all[0:1, q * BANK:(q + 1) * BANK], start=True,
                          stop=True).then_inc(gain_spread, 1)

            pe.wait_ge(ones_ready, 1)
            pe.wait_ge(gain_landed[0], 16)
            spread_gain(0)
            spread_gain(1)
            pe.wait_ge(ident_ready, 1)
            norm_turn(0, 0)
            spread_gain(2)
            spread_gain(3)
            for b in range(NB):
                pe.wait_ge(norm_lo_ready, b + 1)
                for k in range(2):
                    pe.wait_ge(lo_ready, k + 1)
                    queries_keys(k, b)
                    mm = value_rows(k, b)
                    if b == NB - 1:
                        mm.then_inc(weights_used, 1)
                    elif k == 0:
                        norm_turn(0, 1)
            norm_turn(0, 2)
            norm_turn(0, 3)
            pe.wait_ge(table_landed, 32)
            pe.matmul(psum[0:MAPS, 3, 0:S], table_sb[:, :], onehot_sb, start=True, stop=True).then_inc(table_summed, 1)
            for k in range(2, KC):
                norm_rest(0, k)
                qkv(0, k, first=True)
                if k == CONV_STEP:
                    pe.wait_ge(conv_landed, (TAPS + 1) * 16)
                    pe.wait_ge(table_stored, 1)
                    for t in range(TAPS + 1):
                        mm = turn(psum[:, 3, t * 2 * FC:(t + 1) * 2 * FC], conv_rows[:, t, :], 2 * FC)
                    mm.then_inc(conv_turned, 1)
            with pe.Fori(1, QKV_GROUPS) as g:
                for k in range(KC):
                    qkv(g, k)
                    attention(g - 1, k, QKV_PLAN)
            def o_half(half, step):
                n = half * HEADS + step

                def free(bank):
                    if half == 1:
                        pe.wait_ge(oT_stored, HEADS)
                    elif bank < NB:
                        pe.wait_ge(qk_stored, NB * QKV_GROUPS - NB + bank + 1)
                    elif bank == NB:
                        pe.wait_ge(v_stored, QKV_GROUPS)

                banks = projection_banks(O_FIRST_BANK[half])
                if n == 0:
                    banks = banks[-1:] + banks[:-1]
                project(O_BASE + n, n, step, banks, step == 0, step == HEADS - 1, free)

            for h in range(HEADS):
                o_half(0, h)
                attention(QKV_GROUPS - 1, h, O_PLAN)
            for h in range(HEADS - 2):
                o_half(1, h)
            n = 2 * HEADS - 2
            pe.wait_ge(lo_ready, O_BASE + n + 2)
            pe.wait_ge(chunk_lo_ready, n + 2)
            for i, (bank, b, c) in enumerate(projection_banks(O_FIRST_BANK[1])):
                for h in (HEADS - 2, HEADS - 1):
                    s, tokens = h % SPLIT_SLOTS, slice(b * P, (b + 1) * P)
                    mm = product(psum[:, bank, :], (chunk_hi[:, s, tokens], chunk_lo[:, s, tokens]),
                                 weight_part(h, slice(c * BANK, (c + 1) * BANK)), False, h == HEADS - 1)
                    if i == 2 * NB - 1:
                        mm.then_inc(weights_used, 1)
                    elif h == HEADS - 1:
                        mm.then_inc(proj_summed, 1)
            norm_turn(1, 0)
            norm_turn(1, 1)
            for k in range(KC):
                if k == 1:
                    norm_turn(1, 2)
                    norm_turn(1, 3)
                norm_rest(1, k)
                ffn_in_first(k)
            with pe.Fori(1, FFN_GROUPS) as g:
                for k in range(KC):
                    ffn_in(g, k)
            def out_chunk(half, c, slot, start=False, stop=False):
                def free(bank):
                    pe.wait_ge(blocks_stored, 2 * FFN_BLOCKS * (FFN_GROUPS - 1) + ffn_bank(bank) + 1)

                project(OUT_BASE + half * FC + c, 2 * HEADS + half * FC + c, slot,
                        projection_banks(OUT_FIRST_BANK[half]), start, stop, free)

            rest = FC % RAW_SLOTS
            for j in range(RAW_SLOTS):
                out_chunk(0, j, j, start=j == 0)
            with pe.Fori(1, FC // RAW_SLOTS) as i:
                for j in range(RAW_SLOTS):
                    out_chunk(0, i * RAW_SLOTS + j, j)
            for j in range(rest):
                out_chunk(0, FC - rest + j, j, stop=j == rest - 1)
            for j in range(rest):
                out_chunk(1, j, rest + j, start=j == 0)
            with pe.Fori(0, FC // RAW_SLOTS - 1) as i:
                for j in range(RAW_SLOTS):
                    out_chunk(1, i * RAW_SLOTS + rest + j, j)
            for j in range(RAW_SLOTS):
                out_chunk(1, FC - RAW_SLOTS + j, j, stop=j == RAW_SLOTS - 1)


INPUTS = ["x", "rel_table", "attn_norm_g", "ffn_norm_g", "da_w_qkv", "da_w_o", "da_q_gain", "da_k_gain",
          "da_lam_q1", "da_lam_k1", "da_lam_q2", "da_lam_k2", "da_sub_gain", "ffn_w_in", "ffn_conv_w",
          "ffn_conv_b", "ffn_w_out"]


def bucket_rows(seq, buckets, max_distance=128):
    import numpy as np

    exact = buckets // 2
    d = np.arange(seq - 1, -1, -1)
    ratio = np.log(np.maximum(d, 1).astype(np.float32) / np.float32(exact)) / np.float32(np.log(max_distance / exact))
    large = np.minimum(exact + (ratio * np.float32(buckets - exact)).astype(np.int32), buckets - 1)
    bucket = np.where(d < exact, d, large)
    return (bucket[None, :] == np.arange(buckets)[:, None]).astype(np.float32)


def kernel(**inputs):
    import numpy as np
    import concourse.bacc as bacc
    from concourse import mybir
    from concourse.bass_utils import run_bass_kernel_spmd

    nc = bacc.Bacc("TRN2", target_bir_lowering=False, num_devices=1)
    arrays = {name: np.ascontiguousarray(inputs[name]) for name in INPUTS}
    arrays["bucket_onehot"] = bucket_rows(inputs["x"].shape[1], inputs["rel_table"].shape[0])
    aps = {name: nc.dram_tensor("in_" + name, a.shape, mybir.dt.from_np(a.dtype), kind="ExternalInput").ap()
           for name, a in arrays.items()}
    out = nc.dram_tensor("result", inputs["x"].shape, mybir.dt.float32, kind="ExternalOutput").ap()
    build_layer(nc, aps["x"], aps["rel_table"], aps["bucket_onehot"], aps["attn_norm_g"], aps["ffn_norm_g"],
                aps["da_w_qkv"], aps["da_w_o"], aps["da_q_gain"], aps["da_k_gain"], aps["da_lam_q1"],
                aps["da_lam_k1"], aps["da_lam_q2"], aps["da_lam_k2"], aps["da_sub_gain"], aps["ffn_w_in"],
                aps["ffn_conv_w"], aps["ffn_conv_b"], aps["ffn_w_out"], out)
    r = run_bass_kernel_spmd(nc, [{"in_" + name: a for name, a in arrays.items()}], core_ids=[0])
    return r.results[0]["result"]
```
